# Optimizing a Trainium2 kernel written in Bass

```python
import math
import jax, jax.numpy as jnp
from jax import lax
import numpy as np

D_MODEL = 1024
BATCH = 1
SEQ = 1024
DEPTH = 1

CHUNK = 64
CONV_DIM = 512
CONV_WIDTH = 31
SB_HEADS = 8
SB_HEAD_DIM = 64
SB_DIM = SB_HEADS * SB_HEAD_DIM
Q_BLOCK = 128
N_BRANCH = 2
PEER_HEADS = 8
PEER_KEY_DIM = 256
PEER_HALF = PEER_KEY_DIM // 2
N_KEYS = 128
N_EXPERTS = N_KEYS * N_KEYS
PEER_TOPK = 16
TOKEN_BLOCK = 128
LN_EPS = 1e-5
DEEPNORM_ALPHA = (2.0 * DEPTH) ** 0.25
DEEPNORM_BETA = (8.0 * DEPTH) ** -0.25

COL_CONV = 0
COL_Q = COL_CONV + 2 * CONV_DIM
COL_K = COL_Q + SB_DIM
COL_V = COL_K + SB_DIM
COL_GATE = COL_V + SB_DIM
IN_COLS = COL_GATE + N_BRANCH * D_MODEL

kernel_name = "hybrid_conv_stickbreak_peer_deepnorm"

def layer_norm(x, g, b):
    xf = x.astype(jnp.float32)
    mu = jnp.mean(xf, axis=-1, keepdims=True)
    var = jnp.mean(jnp.square(xf - mu), axis=-1, keepdims=True)
    y = (xf - mu) * lax.rsqrt(var + LN_EPS) * g.astype(jnp.float32) + b.astype(jnp.float32)
    return y.astype(x.dtype)

def conformer_conv(h_glu, w_dw, b_dw, ln_g, ln_b, w_pw2, b_pw2):
    a, gate = jnp.split(h_glu, 2, axis=-1)
    h = a * jax.nn.sigmoid(gate)
    h = lax.conv_general_dilated(
        h, w_dw[:, None, :], window_strides=(1,),
        padding=[(CONV_WIDTH - 1, 0)],
        dimension_numbers=('NWC', 'WIO', 'NWC'),
        feature_group_count=CONV_DIM) + b_dw
    h = layer_norm(h, ln_g, ln_b)
    h = jax.nn.silu(h)
    return h @ w_pw2 + b_pw2

def stick_breaking_attention(q, k, v):
    B, H, S, dh = q.shape
    nb = S // Q_BLOCK
    qb = q.reshape(B, H, nb, Q_BLOCK, dh).transpose(2, 0, 1, 3, 4)
    kf = k.astype(jnp.float32)
    vf = v.astype(jnp.float32)
    key_pos = jnp.arange(S)
    scale = 1.0 / math.sqrt(dh)

    def block(args):
        qi, i = args
        z = jnp.einsum('bhqd,bhkd->bhqk', qi.astype(jnp.float32), kf) * scale
        q_pos = i * Q_BLOCK + jnp.arange(Q_BLOCK)
        mask = key_pos[None, :] < q_pos[:, None]
        log_beta = jax.nn.log_sigmoid(z)
        log_one_minus = jnp.where(mask, jax.nn.log_sigmoid(-z), 0.0)
        suffix = lax.cumsum(log_one_minus, axis=3, reverse=True) - log_one_minus
        att = jnp.where(mask, jnp.exp(log_beta + suffix), 0.0)
        return jnp.einsum('bhqk,bhkd->bhqd', att, vf)

    out = lax.map(block, (qb, jnp.arange(nb)))
    out = out.transpose(1, 0, 3, 2, 4).reshape(B, S, H * dh)
    return out.astype(q.dtype)

def peer(x, w_q, keys_1, keys_2, expert_u, expert_v):
    B, S, D = x.shape
    xt = x.reshape(-1, TOKEN_BLOCK, D)
    k1 = keys_1.astype(jnp.float32)
    k2 = keys_2.astype(jnp.float32)

    def block(xb):
        q = (xb @ w_q).astype(jnp.float32).reshape(TOKEN_BLOCK, PEER_HEADS, 2, PEER_HALF)
        s1 = jnp.einsum('thd,hkd->thk', q[:, :, 0], k1)
        s2 = jnp.einsum('thd,hkd->thk', q[:, :, 1], k2)
        v1, i1 = lax.top_k(s1, PEER_TOPK)
        v2, i2 = lax.top_k(s2, PEER_TOPK)
        cand_s = (v1[..., :, None] + v2[..., None, :]).reshape(TOKEN_BLOCK, PEER_HEADS, PEER_TOPK * PEER_TOPK)
        cand_i = (i1[..., :, None] * N_KEYS + i2[..., None, :]).reshape(TOKEN_BLOCK, PEER_HEADS, PEER_TOPK * PEER_TOPK)
        top_s, pos = lax.top_k(cand_s, PEER_TOPK)
        idx = jnp.take_along_axis(cand_i, pos, axis=-1)
        gate = jax.nn.softmax(top_s, axis=-1)
        u = expert_u[idx]
        vv = expert_v[idx]
        act = jax.nn.gelu(jnp.einsum('td,thkd->thk', xb, u).astype(jnp.float32), approximate=False)
        return jnp.einsum('thk,thkd->td', (gate * act).astype(xb.dtype), vv)

    out = lax.map(block, xt)
    return out.reshape(B, S, D)

def setup_inputs(seed: int = 0) -> dict:
    key = jax.random.key(seed)
    ks = jax.random.split(key, 24)
    L, D = DEPTH, D_MODEL
    f32 = jnp.float32
    nrm = lambda k, shape, s: jax.random.normal(k, shape, f32) * s

    x = jax.random.normal(ks[0], (BATCH, SEQ, D), f32)
    w_in = nrm(ks[1], (L, D, IN_COLS), D ** -0.5)
    col_scale = jnp.ones((IN_COLS,), f32).at[COL_V:COL_GATE].set(DEEPNORM_BETA)
    w_in = w_in * col_scale
    b_in = nrm(ks[2], (L, IN_COLS), 0.02)
    conv_w_dw = nrm(ks[3], (L, CONV_WIDTH, CONV_DIM), CONV_WIDTH ** -0.5)
    conv_b_dw = nrm(ks[4], (L, CONV_DIM), 0.02)
    conv_ln_g = 1.0 + nrm(ks[5], (L, CONV_DIM), 0.02)
    conv_ln_b = nrm(ks[6], (L, CONV_DIM), 0.02)
    conv_w_pw2 = nrm(ks[7], (L, CONV_DIM, D), DEEPNORM_BETA * CONV_DIM ** -0.5)
    conv_b_pw2 = nrm(ks[8], (L, D), 0.02)
    sb_w_o = nrm(ks[9], (L, SB_DIM, D), DEEPNORM_BETA * SB_DIM ** -0.5)
    w_out = nrm(ks[10], (L, D, D), DEEPNORM_BETA * D ** -0.5)
    b_out = nrm(ks[11], (L, D), 0.02)
    ln1_g = 1.0 + nrm(ks[12], (L, D), 0.02)
    ln1_b = nrm(ks[13], (L, D), 0.02)
    peer_w_q = nrm(ks[14], (L, D, PEER_HEADS * PEER_KEY_DIM), D ** -0.5)
    peer_keys_1 = nrm(ks[15], (L, PEER_HEADS, N_KEYS, PEER_HALF), PEER_HALF ** -0.5)
    peer_keys_2 = nrm(ks[16], (L, PEER_HEADS, N_KEYS, PEER_HALF), PEER_HALF ** -0.5)
    peer_u = nrm(ks[17], (L, N_EXPERTS, D), D ** -0.5)
    peer_v = nrm(ks[18], (L, N_EXPERTS, D), DEEPNORM_BETA)
    ln2_g = 1.0 + nrm(ks[19], (L, D), 0.02)
    ln2_b = nrm(ks[20], (L, D), 0.02)
    return {"x": x, "w_in": w_in, "b_in": b_in,
            "conv_w_dw": conv_w_dw, "conv_b_dw": conv_b_dw,
            "conv_ln_g": conv_ln_g, "conv_ln_b": conv_ln_b,
            "conv_w_pw2": conv_w_pw2, "conv_b_pw2": conv_b_pw2,
            "sb_w_o": sb_w_o, "w_out": w_out, "b_out": b_out,
            "ln1_g": ln1_g, "ln1_b": ln1_b,
            "peer_w_q": peer_w_q, "peer_keys_1": peer_keys_1, "peer_keys_2": peer_keys_2,
            "peer_u": peer_u, "peer_v": peer_v,
            "ln2_g": ln2_g, "ln2_b": ln2_b}

def reference(x, w_in, b_in, conv_w_dw, conv_b_dw, conv_ln_g, conv_ln_b,
              conv_w_pw2, conv_b_pw2, sb_w_o, w_out, b_out, ln1_g, ln1_b,
              peer_w_q, peer_keys_1, peer_keys_2, peer_u, peer_v, ln2_g, ln2_b):
    B, S, D = x.shape
    for l in range(DEPTH):
        h = x @ w_in[l] + b_in[l]
        h_conv = h[..., COL_CONV:COL_Q]
        q = h[..., COL_Q:COL_K].reshape(B, S, SB_HEADS, SB_HEAD_DIM).transpose(0, 2, 1, 3)
        k = h[..., COL_K:COL_V].reshape(B, S, SB_HEADS, SB_HEAD_DIM).transpose(0, 2, 1, 3)
        v = h[..., COL_V:COL_GATE].reshape(B, S, SB_HEADS, SB_HEAD_DIM).transpose(0, 2, 1, 3)
        g_conv = jax.nn.sigmoid(h[..., COL_GATE:COL_GATE + D])
        g_sb = jax.nn.sigmoid(h[..., COL_GATE + D:IN_COLS])

        y_conv = conformer_conv(h_conv, conv_w_dw[l], conv_b_dw[l], conv_ln_g[l], conv_ln_b[l],
                                conv_w_pw2[l], conv_b_pw2[l])
        y_sb = stick_breaking_attention(q, k, v) @ sb_w_o[l]
        mix = (g_conv * y_conv + g_sb * y_sb) @ w_out[l] + b_out[l]
        x = layer_norm(DEEPNORM_ALPHA * x + mix, ln1_g[l], ln1_b[l])

        y_peer = peer(x, peer_w_q[l], peer_keys_1[l], peer_keys_2[l], peer_u[l], peer_v[l])
        x = layer_norm(DEEPNORM_ALPHA * x + y_peer, ln2_g[l], ln2_b[l])
    return x


_drawn_inputs = setup_inputs


def setup_inputs(seed=0):
    import zlib

    import numpy as np

    out = dict(_drawn_inputs(seed))
    spreads = {}
    factors = {'b_in': 3.204,
     'conv_b_dw': 3.484,
     'conv_ln_g': 4.199,
     'conv_ln_b': 4.323,
     'conv_b_pw2': 2.834,
     'ln2_g': 2.836,
     'ln2_b': 2.949}
    for name, (base, spread) in spreads.items():
        noise = np.random.default_rng([zlib.crc32(name.encode()), seed]).standard_normal(out[name].shape)
        drawn = base * np.exp(spread * noise) if base else spread * noise
        out[name] = __import__('jax').numpy.asarray(drawn.astype(out[name].dtype))
    for name, factor in factors.items():
        out[name] = (out[name] * factor).astype(out[name].dtype)
    return out
```

```python
import math
from contextlib import ExitStack

import concourse.bass as bass
from concourse import mybir

F32 = mybir.dt.float32
BF16 = mybir.dt.bfloat16
U32 = mybir.dt.uint32
ALU = mybir.AluOpType
ACT = mybir.ActivationFunctionType
AX_X = mybir.AxisListType.X

P = 128
D = 1024
S = 1024
KD = D // P
NB = S // P
HALF = 512
CONV = 512
CC = CONV // P
TAPS = 31
PAD = TAPS - 1
HEADS = 8
DH = 64
PAIRS = HEADS // 2
PH = 8
NKEY = 128
TOPK = 16
NEG = -3.0e38
EPS = 1e-5
ALPHA = 2.0 ** 0.25
RING = 8
DIAGS = 4
START = 1
KB = 256

C_A, C_G, C_Q, C_K = 0, CC, 2 * CC, 3 * CC
C_GA, C_GB, C_PW = 4 * CC, 4 * CC + KD, 4 * CC + 2 * KD
C_CB = 4 * CC + 3 * KD
C_LG, C_LB = C_CB + CC, C_CB + 2 * CC
C_CW = C_CB + 3 * CC
N_COLS = C_CW + CC * TAPS


class Steps:

    def __init__(self, eng, sem, base=0, started=None):
        self.eng, self.sem, self.base, self.n, self.started = eng, sem, base, 0, started

    def link(self, ins):
        ins.then_inc(self.sem, 1)
        self.n += 1
        if self.started is None:
            self.eng.wait_ge(self.sem, self.base + self.n)
        else:
            wait_alone(self.eng, self.sem, self.base + self.n, self.started)


def wait_alone(eng, sem, value, started):
    value = eng.to_reg(value)
    eng.wait_ge(started, 1)
    eng.wait_ge(sem, value)


def attention_units():
    return [(Q, kb, hd) for Q in range(S // HALF) for kb in range(4 * Q + 3, -1, -1) for hd in range(2)]


UNITS = attention_units()
NU = len(UNITS)
DIAG_NO = {u: n for n, u in enumerate(u for u, (Q, kb, _) in enumerate(UNITS) if kb >= 4 * Q)}
ACC_NO = {u: n for n, u in enumerate(u for u, (Q, kb, _) in enumerate(UNITS) if kb > 0)}
N_DIAG, N_ACC = len(DIAG_NO), len(ACC_NO)


def build(nc, xT_d, x_d, w_proj_d, w_v_d, w_mix_d, w_out_d, w_q_d, keys_d, uv_d, cols_d, bv_d,
          b_out_d, ln1_g_d, ln1_b_d, ln2_g_d, ln2_b_d, out_d):
    ctx = ExitStack()
    with ctx:
        def sem(name):
            return ctx.enter_context(nc.semaphore(name))

        arena = ctx.enter_context(nc.sbuf_tensor("arena", [P, 205 * KB], F32))

        def at(kib, *shape):
            n = math.prod(shape)
            flat = arena[:, int(kib * KB):int(kib * KB) + n]
            if len(shape) == 1:
                return flat
            if len(shape) == 2:
                return flat.rearrange("p (a b) -> p a b", b=shape[1])
            return flat.rearrange("p (a b c) -> p a b c", b=shape[1], c=shape[2])

        xT = at(0, KD, S)
        x1 = at(0, NB, D)
        qT = at(32, PAIRS, S)
        kT = at(48, PAIRS, S)
        mixT = at(32, KD, S)
        v_sb = at(64, NB, HALF)
        gate_tmp = at(64, 2, 2, HALF)
        w_v = at(80, KD, HALF)
        attT = at(80, PAIRS, S)
        conv = at(96, CC, S)
        conv_in = at(112, CC, S + PAD)
        conv_sq = at(112, CC, S)
        k_pair = at(112, S)
        q_pair = at(120, 2, S)
        v_pair = at(116, NB, P)
        w_ring = at(129, 4, KD, P)
        w_mix = at(129, 2, 3 * D)
        x_in = at(129, 2, D)
        pre = at(137, D)
        mix_blk = at(141, 2, KD, P)
        glu_gate = at(153, 2, S)
        rstd_row = at(161, S)
        el = at(153, 4, HALF)
        sp = at(161, 3, HALF)
        att = at(167, 3, HALF)
        acc = at(173, 2, 2, HALF)
        w_out = at(153, KD, D)
        b_out_bc = at(185, D)
        ln1_g_bc = at(189, D)
        ln1_b_bc = at(193, D)
        keysT = at(197, PH, 2, NKEY)
        x1T = at(32, KD, P)
        ln2_g_bc = at(36, D)
        ln2_b_bc = at(40, D)
        pre2 = at(44, D)
        q_sb = at(48, 2, P)
        score = at(49, 2, NKEY)
        cand = at(50, TOPK, TOPK)
        onehot = at(51, TOPK, 2 * TOPK)
        x1_blk = at(53, D)
        q_nat = at(63, 2 * P)
        gates = at(57, NB, PH * TOPK)
        w_q = at(64, KD, PH * 2 * P)
        ring = at(128, RING, 2 * D)
        idx_f = at(192, TOPK)
        top_v = at(192.25, 2, TOPK)
        soft = at(193, TOPK)

        def small(name, shape, dt=F32):
            return ctx.enter_context(nc.sbuf_tensor(name, [P] + shape, dt))

        cols = small("cols", [N_COLS])
        q_bias8 = small("q_bias8", [CC])
        ident = at(194, P)
        tri = at(184, P)
        neg_ones = at(184.5, P)
        mean_w = at(181, P)
        bv_row = at(181.5, HALF)
        one_row = at(183.5, P)
        gates_flat = gates.rearrange("p a b -> p (a b)")
        zeros = small("zeros", [HALF], BF16)
        stats = small("stats", [2, 6])
        mv = small("mv", [2])
        std = small("std", [1])
        eps_col = small("eps_col", [1])
        rstd = small("rstd", [1])
        hcol = small("hcol", [TOPK])
        gcol = small("gcol", [TOPK])
        wcol = small("wcol", [TOPK])
        diag = at(195, DIAGS, P)
        idx_now = small("idx_now", [TOPK], U32)
        top_i = small("top_i", [2, TOPK], U32)
        pos = small("pos", [TOPK], U32)
        pos_ab = small("pos_ab", [TOPK, 2], U32)
        iota16 = small("iota16", [TOPK])
        iota_i = small("iota_i", [TOPK], mybir.dt.int32)
        top_s = small("top_s", [TOPK])
        den = small("den", [1])
        rden = small("rden", [1])

        ps = ctx.enter_context(nc.psum_tensor("ps", [P, 8, HALF], F32))
        ps_flat = ps[:, :, :].rearrange("p a b -> p (a b)")

        xT_in = [sem(f"xT_in{k}") for k in range(KD)]
        cols_in = sem("cols_in")
        w_in = [sem(f"w_in{j}") for j in range(4)]
        wv_in = sem("wv_in")
        bv_in = sem("bv_in")
        proj_done = sem("proj_done")
        psum_read = [sem(f"psum_read{j}") for j in range(4)]
        v_done = sem("v_done")
        qb_ready = sem("qb_ready")
        sig_ready = sem("sig_ready")
        conv_step = sem("conv_step")
        conv_done = sem("conv_done")
        pad_ready = sem("pad_ready")
        consts = sem("consts")
        pool_step = sem("pool_step")
        mean_done = sem("mean_done")
        centred = sem("centred")
        squared = sem("squared")
        k_staged = sem("k_staged")
        v_staged = sem("v_staged")
        blk_staged = sem("blk_staged")
        q_zeroed = sem("q_zeroed")
        x1_staged = sem("x1_staged")
        qT_psum = sem("qT_psum")
        qT_ready = sem("qT_ready")
        var_done = sem("var_done")
        std_done = sem("std_done")
        rstd_done = sem("rstd_done")
        normed = sem("normed")
        swish_done = sem("swish_done")
        z_done = sem("z_done")
        abs_done = sem("abs_done")
        e_done = sem("e_done")
        l_done = sem("l_done")
        sp_done = sem("sp_done")
        sp_masked = sem("sp_masked")
        acc_done = sem("acc_done")
        suffix_done = sem("suffix_done")
        att_done = sem("att_done")
        att_masked = sem("att_masked")
        av_done = sem("av_done")
        out_read = sem("out_read")
        wmix_in = [sem(f"wmix_in{j}") for j in range(2)]
        gates_done = sem("gates_done")
        branch_done = sem("branch_done")
        sigs_ready = sem("sigs_ready")
        mix_step = sem("mix_step")
        mixed = [sem(f"mixed{j}") for j in range(2)]
        wout_in = sem("wout_in")
        rows_in = sem("rows_in")
        x_loaded = [sem(f"x_loaded{j}") for j in range(2)]
        wout_done = sem("wout_done")
        pre_read = [sem(f"pre_read{j}") for j in range(2)]
        ln1_step = sem("ln1_step")
        var1_ready = sem("var1_ready")
        std1_ready = sem("std1_ready")
        x1_ready = sem("x1_ready")
        wq_in = sem("wq_in")
        keys_in = sem("keys_in")
        rows2_in = sem("rows2_in")
        x1T_psum = sem("x1T_psum")
        x1T_ready = sem("x1T_ready")
        q_psum = sem("q_psum")
        q_ready = sem("q_ready")
        score_psum = sem("score_psum")
        score_ready = sem("score_ready")
        topk_step = sem("topk_step")
        idx_ready = sem("idx_ready")
        soft_step = sem("soft_step")
        shifted = sem("shifted")
        exp_ready = sem("exp_ready")
        gates_ready = sem("gates_ready")
        gathered = [sem(f"gathered{r}") for r in range(RING)]
        dots_done = sem("dots_done")
        gelu_step = sem("gelu_step")
        diag_ready = sem("diag_ready")
        expert_used = [sem(f"expert_used{r}") for r in range(RING)]
        y_read = sem("y_read")
        ln2_step = sem("ln2_step")
        var2_ready = sem("var2_ready")
        std2_ready = sem("std2_ready")
        out_ready = sem("out_ready")
        eps_ready = sem("eps_ready")
        iota_ready = sem("iota_ready")
        idx_copied = sem("idx_copied")
        stored = sem("stored")

        block = ctx.enter_context(nc.Block())

        TOPK_STEPS = 19

        @block.sync
        def _(sp_eng):
            sp_eng.dma_start(w_ring[:, 0, :, :].rearrange("p a b -> p (a b)"), w_proj_d[0, :, :]).then_inc(w_in[0], 16)
            for k in range(KD):
                sp_eng.dma_start(xT[:, k, :], xT_d[:, k, :]).then_inc(xT_in[k], 16)
            sp_eng.dma_start(cols[:, :], cols_d).then_inc(cols_in, 16)
            for j in range(1, 4):
                sp_eng.dma_start(w_ring[:, j, :, :].rearrange("p a b -> p (a b)"), w_proj_d[j, :, :]).then_inc(w_in[j], 16)
            sp_eng.dma_start(w_v, w_v_d).then_inc(wv_in, 16)
            sp_eng.dma_start(bv_row[0:1, :], bv_d).then_inc(bv_in, 16)
            sp_eng.dma_start(keysT.rearrange("p a b c -> p (a b c)"), keys_d).then_inc(keys_in, 16)
            with sp_eng.Fori(1, 4) as it:
                for j in range(4):
                    sp_eng.wait_ge(proj_done, (it - 1) * 4 + j + 1)
                    sp_eng.dma_start(w_ring[:, j, :, :].rearrange("p a b -> p (a b)"),
                                     w_proj_d[it * 4 + j, :, :]).then_inc(w_in[j], 16)
            sp_eng.wait_ge(proj_done, 16)
            for j in range(2):
                sp_eng.dma_start(w_mix[:, j, :], w_mix_d[j, :, :]).then_inc(wmix_in[j], 16)
            sp_eng.wait_ge(out_read, START + PAIRS * 2)
            sp_eng.dma_start(w_out, w_out_d).then_inc(wout_in, 16)
            sp_eng.dma_start(b_out_bc, b_out_d.partition_broadcast(P)).then_inc(rows_in, 16)
            sp_eng.dma_start(ln1_g_bc, ln1_g_d.partition_broadcast(P)).then_inc(rows_in, 16)
            sp_eng.dma_start(ln1_b_bc, ln1_b_d.partition_broadcast(P)).then_inc(rows_in, 16)
            with sp_eng.Fori(1, 4) as it:
                for j in range(2):
                    sp_eng.wait_ge(branch_done, it * 4 + 2 * j - 2)
                    sp_eng.dma_start(w_mix[:, j, :], w_mix_d[it * 2 + j, :, :]).then_inc(wmix_in[j], 16)
            sp_eng.wait_ge(branch_done, 2 * KD)
            for j in range(2):
                sp_eng.dma_start(x_in[:, j, :], x_d[j * P:(j + 1) * P, :]).then_inc(x_loaded[j], 16)
            for j in range(2):
                sp_eng.wait_ge(mixed[j], START + KD)
            sp_eng.dma_start(w_q, w_q_d).then_inc(wq_in, 16)
            with sp_eng.Fori(1, NB // 2) as i:
                for j in range(2):
                    sp_eng.wait_ge(pre_read[j], START + i)
                    sp_eng.dma_start(x_in[:, j, :], x_d[bass.ds((i * 2 + j) * P, P), :]).then_inc(x_loaded[j], 16)
            sp_eng.wait_ge(wout_done, NB)
            sp_eng.dma_start(ln2_g_bc, ln2_g_d.partition_broadcast(P)).then_inc(rows2_in, 16)
            sp_eng.dma_start(ln2_b_bc, ln2_b_d.partition_broadcast(P)).then_inc(rows2_in, 16)
            with sp_eng.Fori(0, NB) as b:
                sp_eng.wait_ge(out_ready, b + 1)
                sp_eng.dma_start(out_d[bass.ds(b * P, P), :], pre2).then_inc(stored, 16)
            sp_eng.wait_ge(stored, 16 * START + 16 * NB)

        @block.gpsimd
        def _(pool):
            for s in (psum_read + expert_used + mixed + pre_read +
                      [att_done, sp_done, suffix_done, av_done, acc_done, out_read, z_done, x1_ready, q_ready,
                       qT_ready, score_ready, y_read, idx_ready, idx_copied, x1T_psum]):
                pool.sem_inc(s, START)
            pool.sem_inc(stored, 16 * START)
            pool.memset(conv_in[:, :, 0:PAD], 0.0).then_inc(pad_ready, 1)
            pool.memset(mean_w, 1.0 / CONV).then_inc(consts, 1)
            pool.memset(one_row[0:1, :], 1.0).then_inc(consts, 1)
            pool.memset(neg_ones, -1.0).then_inc(consts, 1)
            pool.memset(zeros[:, :], 0.0).then_inc(consts, 1)
            pool.memset(tri, -1.0).then_inc(pool_step, 1)
            pool.iota(iota_i[:, :], pattern=[[1, TOPK]], base=0, channel_multiplier=0).then_inc(consts, 1)
            pool.wait_ge(pool_step, 1)
            pool.affine_select(out=tri, in_=tri, compare_op=ALU.is_ge, fill=0.0, base=0,
                               pattern=[[-1, P]], channel_multiplier=1).then_inc(consts, 1)

            pool.wait_ge(var_done, 1)
            pool.memset(q_pair[DH:P, 0, :], 0.0).then_inc(q_zeroed, 1)
            pool.memset(q_pair[0:DH, 1, :], 0.0).then_inc(q_zeroed, 1)
            with pool.Fori(0, PAIRS) as p:
                order = sorted([(u, 0) for u in DIAG_NO] + [(u + 1.5, 1) for u in DIAG_NO])
                for key, what in order:
                    u = int(key) if what == 0 else int(key - 1.5)
                    Q, kb, hd = UNITS[u]
                    c0 = kb * P - Q * HALF
                    if what == 0:
                        wait_alone(pool, sp_done, START + p * NU + u + 1, consts)
                        tile, signal = sp[:, u % 3, c0:c0 + P], sp_masked
                    else:
                        wait_alone(pool, att_done, START + p * NU + u + 1, consts)
                        tile, signal = att[:, u % 3, c0:c0 + P], att_masked
                    pool.affine_select(out=tile, in_=tile, compare_op=ALU.is_gt, fill=0.0, base=0,
                                       pattern=[[1, P]], channel_multiplier=-1).then_inc(signal, 1)

            pool.wait_ge(x1_ready, START + NB)
            pool.memset(ident, 0.0).then_inc(pool_step, 1)
            pool.wait_ge(pool_step, 2)
            pool.affine_select(out=ident, in_=ident, compare_op=ALU.not_equal, fill=1.0, base=0,
                               pattern=[[-1, P]], channel_multiplier=1).then_inc(consts, 1)

            with pool.Fori(0, NB * PH) as t:
                wait_alone(pool, idx_ready, START + t + 1, consts)
                for s in range(TOPK):
                    if s % RING == 0:
                        pool.tensor_copy(idx_now[:, s:s + RING],
                                         idx_f[:, s:s + RING]).then_inc(idx_copied, 1)
                        wait_alone(pool, idx_copied, START + t * 2 + (s // RING + 1), consts)
                    wait_alone(pool, expert_used[s % RING], START + t * 2 + s // RING, consts)
                    pool.indirect_dma_start(
                        out=ring[:, s % RING, :], out_offset=None, in_=uv_d,
                        in_offset=bass.IndirectOffsetOnAxis(ap=idx_now[:, s:s + 1], axis=0),
                    ).then_inc(gathered[s % RING], 16)

        @block.tensor
        def _(pe):
            pe.wait_ge(consts, 6)

            with pe.Fori(0, 4) as it:
                for j in range(4):
                    pe.wait_ge(w_in[j], (it + 1) * 16)
                    pe.wait_ge(psum_read[j], START + it)
                    for k in range(KD):
                        if j == 0:
                            pe.wait_ge(xT_in[k], 16)
                        for h in range(2):
                            last = nc.tensor.matmul(ps[:, 2 * j + h, :], w_ring[:, j, k, :],
                                                    xT[:, k, h * HALF:(h + 1) * HALF],
                                                    start=(k == 0), stop=(k == KD - 1))
                    last.then_inc(proj_done, 1)
            pe.wait_ge(wv_in, 16)
            pe.wait_ge(bv_in, 16)
            for b in range(NB):
                j = b % 4
                pe.wait_ge(psum_read[j], START + b // 4 + 4)
                nc.tensor.matmul(ps[:, 2 * j, :], one_row[0:1, :], bv_row[0:1, :], start=True, stop=False)
                for k in range(KD):
                    last = nc.tensor.matmul(ps[:, 2 * j, :], xT[:, k, b * P:(b + 1) * P],
                                            w_v[:, k, :], start=False, stop=(k == KD - 1))
                last.then_inc(v_done, 1)

            pe.wait_ge(conv_done, CC)
            pe.wait_ge(psum_read[0], START + 6)
            for h in range(2):
                for c in range(CC):
                    last = nc.tensor.matmul(ps[:, h, :], mean_w, conv[:, c, h * HALF:(h + 1) * HALF],
                                            start=(c == 0), stop=(c == CC - 1))
            last.then_inc(mean_done, 1)
            pe.wait_ge(psum_read[1], START + 6)
            for c in range(CC):
                pe.wait_ge(squared, c + 1)
                for h in range(2):
                    last = nc.tensor.matmul(ps[:, 2 + h, :], mean_w, conv_sq[:, c, h * HALF:(h + 1) * HALF],
                                            start=(c == 0), stop=(c == CC - 1))
            last.then_inc(var_done, 1)

            pe.wait_ge(std_done, 1)
            pe.wait_ge(psum_read[2], START + 6)
            pe.wait_ge(psum_read[3], START + 6)

            def score_mm(p, u):
                Q, kb, hd = UNITS[u]
                c0 = max(0, kb * P - Q * HALF)
                pe.wait_ge(att_done, START + p * NU + (u - 3 if u >= 4 else 0))
                nc.tensor.matmul(ps[:, u % 4, c0:HALF], k_pair[:, kb * P:(kb + 1) * P],
                                 q_pair[:, hd, Q * HALF + c0:(Q + 1) * HALF],
                                 start=True, stop=True, skip_group_check=True).then_inc(z_done, 1)

            def suffix_mm(p, u):
                Q, kb, hd = UNITS[u]
                c0 = max(0, kb * P - Q * HALF)
                diagonal = kb >= 4 * Q
                old = c0 + P if diagonal else 0
                if diagonal:
                    pe.wait_ge(sp_masked, p * N_DIAG + DIAG_NO[u] + 1)
                else:
                    pe.wait_ge(sp_done, START + p * NU + u + 1)
                first = kb == 4 * Q + 3
                last = nc.tensor.matmul(ps[:, u % 4, c0:HALF], tri, sp[:, u % 3, c0:HALF],
                                        start=False, stop=True, skip_group_check=True)
                if not first:
                    pe.wait_ge(acc_done, START + p * N_ACC + ACC_NO[u - 2] + 1)
                    last = nc.tensor.matmul(ps[:, u % 4, old:HALF], neg_ones, acc[:, hd, (kb + 1) % 2, old:HALF],
                                            start=False, stop=True, skip_group_check=True)
                last.then_inc(suffix_done, 1)

            def value_mm(p, u):
                Q, kb, hd = UNITS[u]
                c0 = max(0, kb * P - Q * HALF)
                first = kb == 4 * Q + 3
                if kb >= 4 * Q:
                    pe.wait_ge(att_masked, p * N_DIAG + DIAG_NO[u] + 1)
                else:
                    pe.wait_ge(att_done, START + p * NU + u + 1)
                if first and hd == 0:
                    pe.wait_ge(out_read, START + p * 2)
                r = slice(hd * DH, (hd + 1) * DH)
                nc.tensor.matmul(ps[r, 4 + Q, c0:HALF], v_pair[:, kb, hd * DH:(hd + 1) * DH],
                                 att[:, u % 3, c0:HALF],
                                 start=first, stop=(kb == 0), skip_group_check=True).then_inc(av_done, 1)

            with pe.Fori(0, PAIRS) as p:
                pe.wait_ge(k_staged, p + 1)
                for u in range(3):
                    score_mm(p, u)
                pe.wait_ge(v_staged, p + 1)
                for t in range(NU + 1):
                    if t + 3 < NU:
                        score_mm(p, t + 3)
                    if t < NU:
                        suffix_mm(p, t)
                    if t >= 1:
                        value_mm(p, t - 1)

            pe.wait_ge(swish_done, CC)
            pe.wait_ge(out_read, START + PAIRS * 2)
            with pe.Fori(0, KD // 2) as i:
                for j in range(2):
                    pe.wait_ge(wmix_in[j], (i + 1) * 16)
                    for h in range(2):
                        cs = slice(h * HALF, (h + 1) * HALF)
                        pe.wait_ge(mixed[h], START + i * 2 + j)
                        for g in range(2):
                            for k in range(KD):
                                last = nc.tensor.matmul(ps[:, 4 * h + g, :],
                                                        w_mix[:, j, g * D + k * P:g * D + (k + 1) * P],
                                                        xT[:, k, cs], start=(k == 0), stop=(k == KD - 1))
                        last.then_inc(gates_done, 1)
                        for y, src in ((0, conv), (1, attT)):
                            for k in range(CC):
                                o = 2 * D + y * HALF + k * P
                                last = nc.tensor.matmul(ps[:, 4 * h + 2 + y, :], w_mix[:, j, o:o + P],
                                                        src[:, k, cs], start=(k == 0), stop=(k == CC - 1))
                        last.then_inc(branch_done, 1)

            for h in range(2):
                pe.wait_ge(mixed[h], START + KD)
            pe.wait_ge(wout_in, 16)
            with pe.Fori(0, NB // 2) as i:
                for j in range(2):
                    pe.wait_ge(blk_staged, i * 2 + j + 1)
                    pe.wait_ge(pre_read[j], START + i)
                    for k in range(KD):
                        for h in range(2):
                            last = nc.tensor.matmul(ps[:, 4 * j + h, :], mix_blk[:, j, k, :],
                                                    w_out[:, k, h * HALF:(h + 1) * HALF],
                                                    start=(k == 0), stop=(k == KD - 1))
                    last.then_inc(wout_done, 1)

            pe.wait_ge(consts, 7)
            for j in range(2):
                pe.wait_ge(pre_read[j], START + NB // 2)

            def transposes(b):
                pe.wait_ge(x1_staged, b + 1)
                for k in range(KD):
                    last = nc.tensor.transpose(ps_flat[:, k * P:(k + 1) * P], x1_blk[:, k * P:(k + 1) * P], ident)
                last.then_inc(x1T_psum, 1)

            def queries(r, h):
                pe.wait_ge(q_ready, START + r)
                for k in range(KD):
                    last = nc.tensor.matmul(ps[:, 2, 0:2 * P], x1T[:, k, :], w_q[:, k, bass.ds(h * 2 * P, 2 * P)],
                                            start=(k == 0), stop=(k == KD - 1))
                last.then_inc(q_psum, 1)

            def query_transposes(r):
                pe.wait_ge(q_ready, START + r + 1)
                pe.wait_ge(qT_ready, START + r)
                for half in range(2):
                    last = nc.tensor.transpose(ps[:, 6, half * P:(half + 1) * P],
                                               q_nat[:, half * P:(half + 1) * P], ident)
                last.then_inc(qT_psum, 1)

            def scores(r, h):
                pe.wait_ge(qT_ready, START + r + 1)
                pe.wait_ge(score_ready, START + r)
                for half in range(2):
                    last = nc.tensor.matmul(ps[:, 3, half * P:(half + 1) * P], q_sb[:, half, :],
                                            keysT[:, h, half, :], start=True, stop=True)
                last.then_inc(score_psum, 1)

            def experts(t, g):
                for s in range(2 * g, 2 * g + 2):
                    pe.wait_ge(diag_ready, t * TOPK + s + 1)
                    for h in range(2):
                        last = nc.tensor.matmul(ps[:, 4 + h, :], diag[:, s % DIAGS, :],
                                                ring[:, s % RING, D + h * HALF:D + (h + 1) * HALF],
                                                start=False, stop=False, skip_group_check=True)
                    last.then_inc(expert_used[s % RING], 1)

            def clear_y(b):
                pe.wait_ge(y_read, START + b)
                for h in range(2):
                    nc.tensor.matmul(ps[:, 4 + h, :], zeros[:, 0:P], zeros[:, :], start=True, stop=True,
                                     skip_group_check=True)

            def experts_and_retrieval(t, r, h):
                for g in range(TOPK // 2):
                    if r is not None and g == 0:
                        queries(r, h)
                    if r is not None and g == 1:
                        query_transposes(r)
                    if r is not None and g == 2:
                        scores(r, h)
                    experts(t, g)

            pe.wait_ge(wq_in, 16)
            pe.wait_ge(keys_in, 16)
            transposes(0)
            pe.wait_ge(x1T_ready, 1)
            queries(0, 0)
            query_transposes(0)
            scores(0, 0)
            with pe.Fori(0, NB - 1) as b:
                clear_y(b)
                with pe.Fori(0, PH - 1) as h:
                    experts_and_retrieval(b * PH + h, b * PH + h + 1, h + 1)
                transposes(b + 1)
                wait_alone(pe, x1T_ready, b + 2, consts)
                experts_and_retrieval(b * PH + (PH - 1), b * PH + PH, 0)
            clear_y(NB - 1)
            with pe.Fori(0, PH - 1) as h:
                experts_and_retrieval(h + (NB - 1) * PH, h + ((NB - 1) * PH + 1), h + 1)
            experts_and_retrieval(NB * PH - 1, None, None)

        @block.scalar
        def _(act):
            act.wait_ge(cols_in, 16)
            act.wait_ge(eps_ready, 1)
            nc.scalar.mul(q_bias8[:, :], cols[:, C_Q:C_Q + CC], DH ** -0.5).then_inc(qb_ready, 1)
            with act.Fori(0, 2) as it:
                for j in (1, 3):
                    act.wait_ge(proj_done, it * 4 + j + 1)
                    act.wait_ge(psum_read[j - 1], START + it)
                    nc.scalar.activation(glu_gate[:, j // 2, :], ps_flat[:, j * 2 * HALF:(j + 1) * 2 * HALF],
                                         ACT.Sigmoid, bias=cols[:, bass.ds(it * 2 + (C_G + j // 2), 1)]
                                         ).then_inc(psum_read[j], 1)
            act.wait_ge(qb_ready, 1)
            for j in range(4):
                act.wait_ge(proj_done, 8 + j + 1)
                nc.scalar.activation(qT[:, j, :], ps_flat[:, j * 2 * HALF:(j + 1) * 2 * HALF], ACT.Identity,
                                     bias=q_bias8[:, j:j + 1], scale=DH ** -0.5).then_inc(psum_read[j], 1)
            for j in range(4):
                act.wait_ge(proj_done, 12 + j + 1)
                nc.scalar.activation(kT[:, j, :], ps_flat[:, j * 2 * HALF:(j + 1) * 2 * HALF], ACT.Identity,
                                     bias=cols[:, C_K + j:C_K + j + 1]).then_inc(psum_read[j], 1)
            with act.Fori(0, 2) as tt:
                for j in range(4):
                    act.wait_ge(v_done, tt * 4 + j + 1)
                    nc.scalar.activation(v_sb[:, tt * 4 + j, :], ps[:, 2 * j, :], ACT.Copy).then_inc(psum_read[j], 1)

            for c in range(CC):
                act.wait_ge(centred, c + 1)
                nc.scalar.activation(conv_sq[:, c, :], conv[:, c, :], ACT.Square).then_inc(squared, 1)
            act.wait_ge(var_done, 1)
            nc.scalar.activation(rstd_row, ps_flat[:, 2 * HALF:4 * HALF], ACT.Sqrt,
                                 bias=eps_col[:, :]).then_inc(std_done, 1)
            for c in range(CC):
                act.wait_ge(normed, c + 1)
                nc.scalar.activation(conv[:, c, :], conv[:, c, :], ACT.Silu, bias=cols[:, C_LB + c:C_LB + c + 1],
                                     scale=cols[:, C_LG + c:C_LG + c + 1]).then_inc(swish_done, 1)

            def soft_log(p, u):
                Q, kb, hd = UNITS[u]
                c0 = max(0, kb * P - Q * HALF)
                act.wait_ge(z_done, START + p * NU + u + 1)
                act.wait_ge(sp_done, START + p * NU + (u - 3 if u >= 4 else 0))
                nc.scalar.activation(el[:, u % 4, c0:HALF], ps[:, u % 4, c0:HALF], ACT.Abs).then_inc(abs_done, 1)
                act.wait_ge(abs_done, p * NU + u + 1)
                nc.scalar.activation(el[:, u % 4, c0:HALF], el[:, u % 4, c0:HALF], ACT.Exp, scale=-1.0).then_inc(e_done, 1)
                act.wait_ge(e_done, p * NU + u + 1)
                nc.scalar.activation(el[:, u % 4, c0:HALF], el[:, u % 4, c0:HALF], ACT.Ln, bias=1.0).then_inc(l_done, 1)

            def weights(p, u):
                Q, kb, hd = UNITS[u]
                c0 = max(0, kb * P - Q * HALF)
                act.wait_ge(suffix_done, START + p * NU + u + 1)
                act.wait_ge(av_done, START + p * NU + (u - 2 if u >= 3 else 0))
                nc.scalar.activation(att[:, u % 3, c0:HALF], ps[:, u % 4, c0:HALF], ACT.Exp).then_inc(att_done, 1)

            def evacuate(p, Q, last_unit):
                act.wait_ge(av_done, START + p * NU + last_unit + 1)
                nc.scalar.activation(attT[:, p, Q * HALF:(Q + 1) * HALF], ps[:, 4 + Q, :], ACT.Copy).then_inc(out_read, 1)

            act.preload_act_table_set("natural_log_exp_and_others")
            with act.Fori(0, PAIRS) as p:
                soft_log(p, 0)
                soft_log(p, 1)
                for t in range(NU):
                    if t + 2 < NU:
                        soft_log(p, t + 2)
                    weights(p, t)
                    if t == 10:
                        evacuate(p, 0, 7)
                evacuate(p, 1, NU - 1)

            with act.Fori(0, KD) as m:
                for h in range(2):
                    act.wait_ge(mixed[h], START + m)
                    wait_alone(act, gates_done, m * 2 + h + 1, cols_in)
                    for g in range(2):
                        nc.scalar.activation(gate_tmp[:, h, g, :], ps[:, 4 * h + g, :], ACT.Sigmoid,
                                             bias=cols[:, bass.ds(m + (C_GA + g * KD), 1)]).then_inc(sigs_ready, 1)
            def stage_mix(b, j):
                nc.scalar.activation(mix_blk[:, j, :, :], mixT[:, :, bass.ds(b * P, P)], ACT.Copy).then_inc(blk_staged, 1)

            for h in range(2):
                act.wait_ge(mixed[h], START + KD)
            def std1(b):
                act.wait_ge(var1_ready, b + 1)
                nc.scalar.activation(std[:, :], mv[:, 1:2], ACT.Sqrt, bias=eps_col[:, :]).then_inc(std1_ready, 1)

            stage_mix(0, 0)
            stage_mix(1, 1)
            with act.Fori(0, NB // 2 - 1) as i:
                for j in range(2):
                    act.wait_ge(wout_done, i * 2 + j + 1)
                    stage_mix(i * 2 + j + 2, j)
                    std1(i * 2 + j)
            std1(NB - 2)
            std1(NB - 1)

            def x1_stage(b):
                act.wait_ge(x1T_psum, START + b)
                nc.scalar.activation(x1_blk, x1[:, b, :], ACT.Copy).then_inc(x1_staged, 1)

            def x1T_out(b):
                act.wait_ge(x1T_psum, START + b + 1)
                nc.scalar.activation(x1T.rearrange("p a b -> p (a b)"), ps_flat[:, 0:D], ACT.Copy).then_inc(x1T_ready, 1)

            def q_out(r):
                act.wait_ge(q_psum, r + 1)
                nc.scalar.activation(q_nat, ps[:, 2, 0:2 * P], ACT.Copy).then_inc(q_ready, 1)

            def qT_out(r):
                act.wait_ge(qT_psum, r + 1)
                nc.scalar.activation(q_sb.rearrange("p a b -> p (a b)"), ps[:, 6, 0:2 * P], ACT.Copy).then_inc(qT_ready, 1)

            def score_out(r):
                act.wait_ge(score_psum, r + 1)
                act.wait_ge(idx_ready, START + r)
                nc.scalar.activation(score.rearrange("p a b -> p (a b)"), ps[:, 3, 0:2 * NKEY],
                                     ACT.Copy).then_inc(score_ready, 1)

            def soft_exp(r):
                act.wait_ge(shifted, r + 1)
                nc.scalar.activation(soft, soft, ACT.Exp, accum_out=den[:, :]).then_inc(exp_ready, 1)

            def expert_weights(t, g, steps):
                act.wait_ge(dots_done, t * (TOPK // 2) + g + 1)
                s0 = 2 * g
                steps.link(nc.scalar.activation(gcol[:, s0:s0 + 2], hcol[:, s0:s0 + 2], ACT.Gelu))
                for s in (s0, s0 + 1):
                    last = nc.scalar.activation(wcol[:, s:s + 1], gcol[:, s:s + 1], ACT.Copy,
                                                scale=gates_flat[:, bass.ds(t * TOPK + s, 1)])
                steps.link(last)
                for s in (s0, s0 + 1):
                    f = s - DIAGS
                    act.wait_ge(expert_used[f % RING], START + t * 2 + (f // RING + 1 if f >= 0 else 0))
                    nc.scalar.activation(diag[:, s % DIAGS, :], ident, ACT.Copy,
                                         scale=wcol[:, s:s + 1]).then_inc(diag_ready, 1)

            def finish_std(b):
                act.wait_ge(var2_ready, b + 1)
                nc.scalar.activation(std[:, :], mv[:, 1:2], ACT.Sqrt, bias=eps_col[:, :]).then_inc(std2_ready, 1)

            def experts_and_retrieval(t, r):
                steps = Steps(act, gelu_step, t * TOPK)
                for g in range(TOPK // 2):
                    if r is not None and g == 0:
                        q_out(r)
                    if r is not None and g == 1:
                        qT_out(r)
                    if r is not None and g == 2:
                        score_out(r)
                    if r is not None and g == 7:
                        soft_exp(r)
                    expert_weights(t, g, steps)
                assert steps.n == TOPK

            act.wait_ge(consts, 7)
            act.wait_ge(x1_ready, START + NB)
            x1_stage(0)
            x1T_out(0)
            q_out(0)
            qT_out(0)
            score_out(0)
            soft_exp(0)
            with act.Fori(0, NB - 1) as b:
                with act.Fori(0, PH - 1) as h:
                    act.wait_ge(gates_ready, b * PH + h + 1)
                    experts_and_retrieval(b * PH + h, b * PH + h + 1)
                x1_stage(b + 1)
                x1T_out(b + 1)
                act.wait_ge(gates_ready, b * PH + PH)
                experts_and_retrieval(b * PH + (PH - 1), b * PH + PH)
                finish_std(b)
            with act.Fori(0, PH - 1) as h:
                act.wait_ge(gates_ready, h + ((NB - 1) * PH + 1))
                experts_and_retrieval(h + (NB - 1) * PH, h + ((NB - 1) * PH + 1))
            act.wait_ge(gates_ready, NB * PH)
            experts_and_retrieval(NB * PH - 1, None)
            finish_std(NB - 1)

        @block.vector
        def _(dve):
            nc.vector.memset(eps_col[:, :], EPS).then_inc(eps_ready, 1)
            dve.wait_ge(cols_in, 16)
            dve.wait_ge(pad_ready, 1)
            with dve.Fori(0, 2) as it:
                for j in (0, 2):
                    dve.wait_ge(proj_done, it * 4 + j + 1)
                    dve.wait_ge(psum_read[j + 1], START + it + 1)
                    nc.vector.scalar_tensor_tensor(
                        out=conv_in[:, it * 2 + j // 2, PAD:PAD + S], in0=ps_flat[:, j * 2 * HALF:(j + 1) * 2 * HALF],
                        scalar=cols[:, bass.ds(it * 2 + (C_A + j // 2), 1)], in1=glu_gate[:, j // 2, :],
                        op0=ALU.add, op1=ALU.mult).then_inc(psum_read[j], 1)
            dve.wait_ge(psum_read[0], START + 2)
            dve.wait_ge(psum_read[2], START + 2)
            with dve.Fori(0, CC) as c:
                steps = Steps(dve, conv_step, c * PAD)
                steps.link(nc.vector.tensor_scalar(conv[:, c, :], conv_in[:, c, 0:S],
                                                   cols[:, bass.ds(c * TAPS + C_CW, 1)],
                                                   cols[:, bass.ds(c + C_CB, 1)], ALU.mult, ALU.add))
                for k in range(1, TAPS):
                    ins = nc.vector.scalar_tensor_tensor(
                        out=conv[:, c, :], in0=conv_in[:, c, k:k + S], scalar=cols[:, bass.ds(c * TAPS + (C_CW + k), 1)],
                        in1=conv[:, c, :], op0=ALU.mult, op1=ALU.add)
                    if k < TAPS - 1:
                        steps.link(ins)
                ins.then_inc(conv_done, 1)
                assert steps.n == PAD
            dve.wait_ge(conv_done, CC)
            dve.wait_ge(mean_done, 1)
            for c in range(CC):
                nc.vector.tensor_tensor(conv[:, c, :], conv[:, c, :], ps_flat[:, 0:2 * HALF],
                                        ALU.subtract).then_inc(centred, 1)
            dve.wait_ge(std_done, 1)
            nc.vector.reciprocal(rstd_row, rstd_row).then_inc(rstd_done, 1)
            dve.wait_ge(rstd_done, 1)
            dve.wait_ge(centred, CC)
            for c in range(CC):
                nc.vector.tensor_tensor(conv[:, c, :], conv[:, c, :], rstd_row, ALU.mult).then_inc(normed, 1)
            dve.wait_ge(normed, CC)

            def softplus(p, u):
                Q, kb, hd = UNITS[u]
                c0 = max(0, kb * P - Q * HALF)
                dve.wait_ge(l_done, p * NU + u + 1)
                dve.wait_ge(suffix_done, START + p * NU + (u - 2 if u >= 3 else 0))
                dve.wait_ge(acc_done, START + p * N_ACC + (sum(v <= u - 3 for v in ACC_NO) if u >= 3 else 0))
                nc.vector.scalar_tensor_tensor(out=sp[:, u % 3, c0:HALF], in0=ps[:, u % 4, c0:HALF], scalar=0.0,
                                               in1=el[:, u % 4, c0:HALF], op0=ALU.max, op1=ALU.add).then_inc(sp_done, 1)

            def accumulate(p, u):
                Q, kb, hd = UNITS[u]
                if kb == 0:
                    return
                c0 = max(0, kb * P - Q * HALF)
                diagonal = kb >= 4 * Q
                old = c0 + P if diagonal else 0
                first = kb == 4 * Q + 3
                if diagonal:
                    dve.wait_ge(sp_masked, p * N_DIAG + DIAG_NO[u] + 1)
                    ins = nc.vector.tensor_copy(acc[:, hd, kb % 2, c0:old], sp[:, u % 3, c0:old])
                else:
                    dve.wait_ge(sp_done, START + p * NU + u + 1)
                if not first:
                    dve.wait_ge(acc_done, START + p * N_ACC + ACC_NO[u - 2] + 1)
                    ins = nc.vector.tensor_tensor(acc[:, hd, kb % 2, old:HALF], acc[:, hd, (kb + 1) % 2, old:HALF],
                                                  sp[:, u % 3, old:HALF], ALU.add)
                ins.then_inc(acc_done, 1)

            dve.wait_ge(psum_read[3], START + 6)
            dve.wait_ge(q_zeroed, 2)
            with dve.Fori(0, PAIRS) as p:
                dve.wait_ge(z_done, START + p * NU)
                nc.vector.tensor_copy(k_pair, kT[:, p, :])
                for hd in range(2):
                    r = slice(hd * DH, (hd + 1) * DH)
                    last = nc.vector.tensor_copy(q_pair[r, hd, :], qT[r, p, :])
                last.then_inc(k_staged, 1)
                dve.wait_ge(av_done, START + p * NU)
                nc.vector.tensor_copy(v_pair, v_sb[:, :, bass.ds(p * P, P)]).then_inc(v_staged, 1)
                softplus(p, 0)
                for t in range(NU):
                    if t + 1 < NU:
                        softplus(p, t + 1)
                    accumulate(p, t)

            with dve.Fori(0, KD) as m:
                for h in range(2):
                    dve.wait_ge(sigs_ready, m * 4 + 2 * h + 2)
                    dve.wait_ge(branch_done, m * 2 + h + 1)
                    nc.vector.scalar_tensor_tensor(out=gate_tmp[:, h, 0, :], in0=ps[:, 4 * h + 2, :],
                                                   scalar=cols[:, bass.ds(m + C_PW, 1)], in1=gate_tmp[:, h, 0, :],
                                                   op0=ALU.add, op1=ALU.mult)
                    nc.vector.tensor_tensor(gate_tmp[:, h, 1, :], ps[:, 4 * h + 3, :], gate_tmp[:, h, 1, :],
                                            ALU.mult).then_inc(mix_step, 1)
                    dve.wait_ge(mix_step, m * 2 + h + 1)
                    nc.vector.tensor_tensor(mixT[:, m, h * HALF:(h + 1) * HALF], gate_tmp[:, h, 0, :],
                                            gate_tmp[:, h, 1, :], ALU.add).then_inc(mixed[h], 1)

            def layer_norm(tile, steps, var_ready, std_ready, turn, g_bc, b_bc, out):
                for h in range(2):
                    last = nc.vector.bn_stats(stats[:, h, :], tile[:, h * HALF:(h + 1) * HALF])
                steps.link(last)
                nc.vector.bn_aggr(mv[:, :], stats[:, :, :].rearrange("p a b -> p (a b)")).then_inc(var_ready, 1)
                dve.wait_ge(std_ready, turn + 1)
                steps.link(nc.vector.reciprocal(rstd[:, :], std[:, :]))
                steps.link(nc.vector.tensor_scalar(tile, tile, mv[:, 0:1], rstd[:, 0:1], ALU.subtract, ALU.mult))
                steps.link(nc.vector.tensor_tensor(tile, tile, g_bc, ALU.mult))
                return nc.vector.tensor_tensor(out, tile, b_bc, ALU.add)

            dve.wait_ge(rows_in, 48)
            with dve.Fori(0, NB // 2) as i:
                for j in range(2):
                    steps = Steps(dve, ln1_step, i * 10 + j * 5, consts)
                    dve.wait_ge(wout_done, i * 2 + j + 1)
                    dve.wait_ge(x_loaded[j], (i + 1) * 16)
                    dve.wait_ge(x1_ready, START + i * 2 + j)
                    nc.vector.scalar_tensor_tensor(out=pre, in0=x_in[:, j, :], scalar=ALPHA,
                                                   in1=ps_flat[:, 4 * j * HALF:(4 * j + 2) * HALF],
                                                   op0=ALU.mult, op1=ALU.add).then_inc(pre_read[j], 1)
                    dve.wait_ge(pre_read[j], START + i + 1)
                    steps.link(nc.vector.tensor_tensor(pre, pre, b_out_bc, ALU.add))
                    layer_norm(pre, steps, var1_ready, std1_ready, i * 2 + j, ln1_g_bc, ln1_b_bc,
                               x1[:, i * 2 + j, :]).then_inc(x1_ready, 1)
                    assert steps.n == 5

            dve.wait_ge(consts, 6)
            nc.vector.tensor_copy(iota16[:, :], iota_i[:, :]).then_inc(iota_ready, 1)
            dve.wait_ge(iota_ready, 1)
            dve.wait_ge(x1_ready, START + NB)

            def topk_half(steps, half):
                s_half = score[:, half, :]
                steps.link(nc.vector.max(top_v[:, half, 0:8], s_half))
                steps.link(nc.vector.max_index(top_i[:, half, 0:8], top_v[:, half, 0:8], s_half))
                steps.link(nc.vector.match_replace(s_half, top_v[:, half, 0:8], s_half, NEG))
                steps.link(nc.vector.max(top_v[:, half, 8:16], s_half))
                steps.link(nc.vector.max_index(top_i[:, half, 8:16], top_v[:, half, 8:16], s_half))

            def topk_pairs(steps, r):
                steps.link(nc.vector.tensor_tensor(cand, top_v[:, 0, :].unsqueeze(2).to_broadcast([P, TOPK, TOPK]),
                                                   top_v[:, 1, :].unsqueeze(1).to_broadcast([P, TOPK, TOPK]), ALU.add))
                cf = cand.rearrange("p a b -> p (a b)")
                g0, g1 = top_s[:, 0:8], top_s[:, 8:16]
                steps.link(nc.vector.max(g0, cf))
                steps.link(nc.vector.max_index(pos[:, 0:8], g0, cf))
                steps.link(nc.vector.match_replace(cf, g0, cf, NEG))
                steps.link(nc.vector.max(g1, cf))
                steps.link(nc.vector.max_index(pos[:, 8:16], g1, cf))
                nc.vector.tensor_scalar(soft, top_s[:, :], top_s[:, 0:1], None, ALU.subtract).then_inc(shifted, 1)

            def expert_index(steps, r):
                nc.vector.tensor_scalar(top_i[:, 0, :], top_i[:, 0, :], 7, None, ALU.logical_shift_left)
                nc.vector.tensor_scalar(pos_ab[:, :, 0], pos[:, :], 4, None, ALU.logical_shift_right)
                steps.link(nc.vector.tensor_scalar(pos_ab[:, :, 1], pos[:, :], 15, None, ALU.bitwise_and))
                oh = onehot.rearrange("p k (a j) -> p k a j", a=2)
                steps.link(nc.vector.tensor_tensor(
                    oh, pos_ab[:, :, :].unsqueeze(3).to_broadcast([P, TOPK, 2, TOPK]),
                    iota16[:, :].unsqueeze(1).unsqueeze(1).to_broadcast([P, TOPK, 2, TOPK]), ALU.is_equal))
                steps.link(nc.vector.tensor_tensor(
                    oh, oh, top_i[:, :, :].unsqueeze(1).to_broadcast([P, TOPK, 2, TOPK]), ALU.mult))
                wait_alone(dve, idx_copied, START + r * 2, consts)
                nc.vector.tensor_reduce(idx_f, onehot, AX_X, ALU.add).then_inc(idx_ready, 1)

            def softmax(r):
                dve.wait_ge(exp_ready, r + 1)
                nc.vector.reciprocal(rden[:, :], den[:, :]).then_inc(soft_step, 1)
                dve.wait_ge(soft_step, r + 1)
                nc.vector.tensor_scalar(gates_flat[:, bass.ds(r * TOPK, TOPK)], soft, rden[:, 0:1], None,
                                        ALU.mult).then_inc(gates_ready, 1)

            def dots(b, t, g):
                for s in range(2 * g, 2 * g + 2):
                    dve.wait_ge(gathered[s % RING], (t * 2 + (s // RING + 1)) * 16)
                    last = nc.vector.scalar_tensor_tensor(
                        out=ring[:, s % RING, 0:D], in0=x1[:, b, :], scalar=1.0, in1=ring[:, s % RING, 0:D],
                        op0=ALU.mult, op1=ALU.mult, accum_out=hcol[:, s:s + 1])
                last.then_inc(dots_done, 1)

            def finish(b):
                steps = Steps(dve, ln2_step, b * 4, consts)
                dve.wait_ge(expert_used[RING - 1], START + b * 2 * PH + 2 * PH)
                dve.wait_ge(expert_used[RING - 2], START + b * 2 * PH + 2 * PH)
                dve.wait_ge(stored, 16 * START + b * 16)
                nc.vector.scalar_tensor_tensor(out=pre2, in0=x1[:, b, :], scalar=ALPHA,
                                               in1=ps_flat[:, 4 * HALF:6 * HALF],
                                               op0=ALU.mult, op1=ALU.add).then_inc(y_read, 1)
                dve.wait_ge(y_read, START + b + 1)
                layer_norm(pre2, steps, var2_ready, std2_ready, b, ln2_g_bc, ln2_b_bc, pre2).then_inc(out_ready, 1)
                assert steps.n == 4

            def experts_and_retrieval(b, t, r):
                steps = Steps(dve, topk_step, r * TOPK_STEPS, consts)
                for g in range(TOPK // 2):
                    dots(b, t, g)
                    if g == 2:
                        wait_alone(dve, score_ready, START + r + 1, consts)
                        topk_half(steps, 0)
                    if g == 3:
                        topk_half(steps, 1)
                    if g == 4:
                        topk_pairs(steps, r)
                    if g == 5:
                        expert_index(steps, r)
                softmax(r)
                assert steps.n == TOPK_STEPS

            steps = Steps(dve, topk_step)
            dve.wait_ge(score_ready, START + 1)
            topk_half(steps, 0)
            topk_half(steps, 1)
            topk_pairs(steps, 0)
            expert_index(steps, 0)
            assert steps.n == TOPK_STEPS, steps.n
            softmax(0)
            dve.wait_ge(rows2_in, 32)
            with dve.Fori(0, NB - 1) as b:
                with dve.Fori(0, PH) as h:
                    experts_and_retrieval(b, b * PH + h, b * PH + h + 1)
                finish(b)
            with dve.Fori(0, PH - 1) as h:
                experts_and_retrieval(NB - 1, h + (NB - 1) * PH, h + ((NB - 1) * PH + 1))
            for g in range(TOPK // 2):
                dots(NB - 1, NB * PH - 1, g)
            finish(NB - 1)


def kernel(x, w_in, b_in, conv_w_dw, conv_b_dw, conv_ln_g, conv_ln_b, conv_w_pw2, conv_b_pw2, sb_w_o,
           w_out, b_out, ln1_g, ln1_b, peer_w_q, peer_keys_1, peer_keys_2, peer_u, peer_v, ln2_g, ln2_b):
    import numpy as np
    import concourse.bacc as bacc
    from concourse.bass_utils import run_bass_kernel_spmd

    def arr(a):
        return np.asarray(a)[0]

    x2, wi, bi = arr(x), arr(w_in), arr(b_in)
    col_q, col_k, col_v, col_g = 1024, 1536, 2048, 2560

    def ktile(w):
        return w.reshape(w.shape[0] // P, P, w.shape[1]).transpose(1, 0, 2)

    def slab(w, c):
        return ktile(w[:, c:c + P]).reshape(P, w.shape[0])

    def col(v):
        return v.reshape(-1, P).T

    order = []
    for c in range(CC):
        order += [c * P, CONV + c * P]
    order += [col_q + c * P for c in range(CC)] + [col_k + c * P for c in range(CC)]
    taps = arr(conv_w_dw).T.reshape(CC, P, TAPS).transpose(1, 0, 2).reshape(P, CC * TAPS)
    data = {
        "xT": ktile(x2.T),
        "x": x2,
        "w_proj": np.stack([slab(wi, c) for c in order]),
        "w_v": ktile(wi[:, col_v:col_g]),
        "w_mix": np.stack([np.concatenate([slab(wi, col_g + m * P), slab(wi, col_g + D + m * P),
                                           slab(arr(conv_w_pw2), m * P), slab(arr(sb_w_o), m * P)], axis=1)
                           for m in range(KD)]),
        "w_out": ktile(arr(w_out)),
        "w_q": ktile(arr(peer_w_q)),
        "keys": np.stack([arr(peer_keys_1), arr(peer_keys_2)], axis=1).transpose(3, 0, 1, 2).reshape(P, PH * 2 * NKEY),
        "uv": np.concatenate([arr(peer_u), arr(peer_v)], axis=1),
        "cols": np.concatenate([col(bi[0:col_v]), col(bi[col_g:]), col(arr(conv_b_pw2)), col(arr(conv_b_dw)),
                                col(arr(conv_ln_g)), col(arr(conv_ln_b)), taps], axis=1),
        "bv": bi[col_v:col_g].reshape(1, -1),
        "b_out": arr(b_out), "ln1_g": arr(ln1_g), "ln1_b": arr(ln1_b), "ln2_g": arr(ln2_g), "ln2_b": arr(ln2_b),
    }
    nc = bacc.Bacc("TRN2", target_bir_lowering=False, num_devices=1)
    arrays, aps = {}, []
    for name, a in data.items():
        a = np.ascontiguousarray(a)
        arrays[f"{name}_dram"] = a
        aps.append(nc.dram_tensor(f"{name}_dram", a.shape, mybir.dt.from_np(a.dtype), kind="ExternalInput").ap())
    out = nc.dram_tensor("out_dram", (S, D), F32, kind="ExternalOutput").ap()
    build(nc, *aps, out)
    r = run_bass_kernel_spmd(nc, [arrays], core_ids=[0])
    return r.results[0]["out_dram"].reshape(1, S, D)
```

```python
import math
from contextlib import ExitStack

import concourse.bass as bass
from concourse import mybir

F32 = mybir.dt.float32
BF16 = mybir.dt.bfloat16
U32 = mybir.dt.uint32
ALU = mybir.AluOpType
ACT = mybir.ActivationFunctionType
AX_X = mybir.AxisListType.X

P = 128
D = 1024
S = 1024
KD = D // P
NB = S // P
HALF = 512
CONV = 512
CC = CONV // P
TAPS = 31
PAD = TAPS - 1
HEADS = 8
DH = 64
PAIRS = HEADS // 2
PH = 8
NKEY = 128
TOPK = 16
NEG = -3.0e38
EPS = 1e-5
ALPHA = 2.0 ** 0.25
RING = 8
DIAGS = 4
START = 1
KB = 256

C_A, C_G, C_Q, C_K = 0, CC, 2 * CC, 3 * CC
C_GA, C_GB, C_PW = 4 * CC, 4 * CC + KD, 4 * CC + 2 * KD
C_CB = 4 * CC + 3 * KD
C_LG, C_LB = C_CB + CC, C_CB + 2 * CC
C_CW = C_CB + 3 * CC
N_COLS = C_CW + CC * TAPS


class Steps:

    def __init__(self, eng, sem, base=0, started=None):
        self.eng, self.sem, self.base, self.n, self.started = eng, sem, base, 0, started

    def link(self, ins):
        ins.then_inc(self.sem, 1)
        self.n += 1
        if self.started is None:
            self.eng.wait_ge(self.sem, self.base + self.n)
        else:
            wait_alone(self.eng, self.sem, self.base + self.n, self.started)


def wait_alone(eng, sem, value, started):
    value = eng.to_reg(value)
    eng.wait_ge(started, 1)
    eng.wait_ge(sem, value)


def attention_units():
    return [(Q, kb, hd) for Q in range(S // HALF) for kb in range(4 * Q + 3, -1, -1) for hd in range(2)]


UNITS = attention_units()
NU = len(UNITS)
DIAG_NO = {u: n for n, u in enumerate(u for u, (Q, kb, _) in enumerate(UNITS) if kb >= 4 * Q)}
ACC_NO = {u: n for n, u in enumerate(u for u, (Q, kb, _) in enumerate(UNITS) if kb > 0)}
N_DIAG, N_ACC = len(DIAG_NO), len(ACC_NO)


def build(nc, xT_d, x_d, w_proj_d, w_v_d, w_mix_d, w_out_d, w_q_d, keys_d, uv_d, cols_d, bv_d,
          b_out_d, ln1_g_d, ln1_b_d, ln2_g_d, ln2_b_d, out_d):
    ctx = ExitStack()
    with ctx:
        def sem(name):
            return ctx.enter_context(nc.semaphore(name))

        arena = ctx.enter_context(nc.sbuf_tensor("arena", [P, 205 * KB], F32))

        def at(kib, *shape):
            n = math.prod(shape)
            flat = arena[:, int(kib * KB):int(kib * KB) + n]
            if len(shape) == 1:
                return flat
            if len(shape) == 2:
                return flat.rearrange("p (a b) -> p a b", b=shape[1])
            return flat.rearrange("p (a b c) -> p a b c", b=shape[1], c=shape[2])

        xT = at(160, KD, S)
        mixT = at(0, NB, KD, P)
        x1 = at(0, NB, D)
        qT = at(32, PAIRS, S)
        kT = at(48, PAIRS, S)
        v_sb = at(64, NB, HALF)
        gate_tmp = at(49, 2, 2, HALF)
        w_v = at(80, KD, HALF)
        attT = at(80, PAIRS, S)
        conv = at(96, CC, S)
        conv_in = at(112, CC, S + PAD)
        conv_sq = at(112, CC, S)
        k_pair = at(112, S)
        q_pair = at(120, 2, S)
        v_pair = at(116, NB, P)
        w_ring = at(129, 4, KD, P)
        w_mix = at(129, 2, 3 * D)
        glu_gate = at(0, 2, S)
        rstd_row = at(8, S)
        el = at(0, 4, HALF)
        sp = at(8, 3, HALF)
        att = at(14, 3, HALF)
        acc = at(20, 2, 2, HALF)
        mean_w = at(28, P)
        bv_row = at(28.5, HALF)
        one_row = at(30.5, P)
        tri = at(31, P)
        neg_ones = at(31.5, P)
        w_out = at(64, KD, D)
        b_out_bc = at(96, D)
        mix_blk = at(100, KD, P)
        x_in = at(104, D)
        ln1_g_bc = at(36, D)
        ln1_b_bc = at(40, D)
        keysT = at(197, PH, 2, NKEY)
        x1T = at(32, KD, P)
        ln2_g_bc = at(36, D)
        ln2_b_bc = at(40, D)
        pre2 = at(44, D)
        q_sb = at(48, 2, P)
        score = at(49, 2, NKEY)
        cand = at(50, TOPK, TOPK)
        onehot = at(51, TOPK, 2 * TOPK)
        x1_blk = at(53, D)
        q_nat = at(63, 2 * P)
        gates = at(57, NB, PH * TOPK)
        w_q = at(64, PH, KD, 2 * P)
        ring = at(128, RING, 2 * D)
        idx_f = at(192, TOPK)
        top_v = at(192.25, 2, TOPK)
        soft = at(193, TOPK)

        def small(name, shape, dt=F32):
            return ctx.enter_context(nc.sbuf_tensor(name, [P] + shape, dt))

        cols = small("cols", [N_COLS])
        q_bias8 = small("q_bias8", [CC])
        ident = at(194, P)
        gates_flat = gates.rearrange("p a b -> p (a b)")
        zeros = small("zeros", [HALF], BF16)
        stats = small("stats", [2, 6])
        mv = small("mv", [2])
        std = small("std", [1])
        eps_col = small("eps_col", [1])
        rstd = small("rstd", [1])
        hcol = small("hcol", [TOPK])
        gcol = small("gcol", [TOPK])
        wcol = small("wcol", [TOPK])
        diag = at(195, DIAGS, P)
        idx_now = small("idx_now", [TOPK], U32)
        top_i = small("top_i", [2, TOPK], U32)
        pos = small("pos", [TOPK], U32)
        pos_ab = small("pos_ab", [TOPK, 2], U32)
        iota16 = small("iota16", [TOPK])
        iota_i = small("iota_i", [TOPK], mybir.dt.int32)
        top_s = small("top_s", [TOPK])
        den = small("den", [1])
        rden = small("rden", [1])

        ps = ctx.enter_context(nc.psum_tensor("ps", [P, 8, HALF], F32))
        ps_flat = ps[:, :, :].rearrange("p a b -> p (a b)")

        xT_in = [sem(f"xT_in{k}") for k in range(KD)]
        cols_in = sem("cols_in")
        w_in = [sem(f"w_in{j}") for j in range(4)]
        wv_in = sem("wv_in")
        bv_in = sem("bv_in")
        proj_done = sem("proj_done")
        psum_read = [sem(f"psum_read{j}") for j in range(4)]
        v_done = sem("v_done")
        qb_ready = sem("qb_ready")
        sig_ready = sem("sig_ready")
        conv_step = sem("conv_step")
        conv_done = sem("conv_done")
        pad_ready = sem("pad_ready")
        consts = sem("consts")
        pool_step = sem("pool_step")
        mean_done = sem("mean_done")
        centred = sem("centred")
        squared = sem("squared")
        k_staged = sem("k_staged")
        v_staged = sem("v_staged")
        blk_staged = sem("blk_staged")
        q_zeroed = sem("q_zeroed")
        x1_staged = sem("x1_staged")
        qT_psum = sem("qT_psum")
        qT_ready = sem("qT_ready")
        var_done = sem("var_done")
        std_done = sem("std_done")
        rstd_done = sem("rstd_done")
        normed = sem("normed")
        swish_done = sem("swish_done")
        z_done = sem("z_done")
        abs_done = sem("abs_done")
        e_done = sem("e_done")
        l_done = sem("l_done")
        sp_done = sem("sp_done")
        sp_masked = sem("sp_masked")
        acc_done = sem("acc_done")
        suffix_done = sem("suffix_done")
        att_done = sem("att_done")
        att_masked = sem("att_masked")
        av_done = sem("av_done")
        out_read = sem("out_read")
        wmix_in = [sem(f"wmix_in{j}") for j in range(2)]
        gates_done = sem("gates_done")
        branch_done = sem("branch_done")
        sigs_ready = sem("sigs_ready")
        mix_step = sem("mix_step")
        mixed = [sem(f"mixed{j}") for j in range(2)]
        wout_in = sem("wout_in")
        rows_in = sem("rows_in")
        x_loaded = sem("x_loaded")
        wout_done = sem("wout_done")
        pre_read = sem("pre_read")
        ln1_step = sem("ln1_step")
        var1_ready = sem("var1_ready")
        std1_ready = sem("std1_ready")
        x1_ready = sem("x1_ready")
        wq_in = sem("wq_in")
        wq0_in = sem("wq0_in")
        wq_rest_in = sem("wq_rest_in")
        keys_in = sem("keys_in")
        rows2_in = sem("rows2_in")
        x1T_psum = sem("x1T_psum")
        x1T_ready = sem("x1T_ready")
        q_psum = sem("q_psum")
        q_ready = sem("q_ready")
        score_psum = sem("score_psum")
        score_ready = sem("score_ready")
        topk_step = sem("topk_step")
        idx_ready = sem("idx_ready")
        soft_step = sem("soft_step")
        shifted = sem("shifted")
        exp_ready = sem("exp_ready")
        gates_ready = sem("gates_ready")
        gathered = [sem(f"gathered{r}") for r in range(RING)]
        dots_done = sem("dots_done")
        gelu_step = sem("gelu_step")
        diag_ready = sem("diag_ready")
        expert_used = [sem(f"expert_used{r}") for r in range(RING)]
        y_read = sem("y_read")
        ln2_step = sem("ln2_step")
        var2_ready = sem("var2_ready")
        std2_ready = sem("std2_ready")
        out_ready = sem("out_ready")
        eps_ready = sem("eps_ready")
        iota_ready = sem("iota_ready")
        idx_copied = sem("idx_copied")
        stored = sem("stored")

        block = ctx.enter_context(nc.Block())

        TOPK_STEPS = 19

        @block.sync
        def _(sp_eng):
            sp_eng.dma_start(w_ring[:, 0, :, :].rearrange("p a b -> p (a b)"), w_proj_d[0, :, :]).then_inc(w_in[0], 16)
            for k in range(KD):
                sp_eng.dma_start(xT[:, k, :], xT_d[:, k, :]).then_inc(xT_in[k], 16)
            sp_eng.dma_start(cols[:, :], cols_d).then_inc(cols_in, 16)
            for j in range(1, 4):
                sp_eng.dma_start(w_ring[:, j, :, :].rearrange("p a b -> p (a b)"), w_proj_d[j, :, :]).then_inc(w_in[j], 16)
            sp_eng.dma_start(w_v, w_v_d).then_inc(wv_in, 16)
            sp_eng.dma_start(bv_row[0:1, :], bv_d).then_inc(bv_in, 16)
            sp_eng.dma_start(keysT.rearrange("p a b c -> p (a b c)"), keys_d).then_inc(keys_in, 16)
            with sp_eng.Fori(1, 4) as it:
                for j in range(4):
                    sp_eng.wait_ge(proj_done, (it - 1) * 4 + j + 1)
                    sp_eng.dma_start(w_ring[:, j, :, :].rearrange("p a b -> p (a b)"),
                                     w_proj_d[it * 4 + j, :, :]).then_inc(w_in[j], 16)
            sp_eng.wait_ge(proj_done, 16)
            for j in range(2):
                sp_eng.dma_start(w_mix[:, j, :], w_mix_d[j, :, :]).then_inc(wmix_in[j], 16)
            sp_eng.wait_ge(out_read, START + PAIRS * 2)
            sp_eng.dma_start(w_out[:, 0:CC, :], w_out_d[:, 0:CC, :]).then_inc(wout_in, 16)
            sp_eng.dma_start(ln1_g_bc, ln1_g_d.partition_broadcast(P)).then_inc(rows_in, 16)
            sp_eng.dma_start(ln1_b_bc, ln1_b_d.partition_broadcast(P)).then_inc(rows_in, 16)
            sp_eng.dma_start(w_q[:, PH - 1, :, :], w_q_d[:, 0, :, :]).then_inc(wq_in, 16)
            sp_eng.dma_start(w_q[:, PH - 2, :, :], w_q_d[:, PH - 2, :, :]).then_inc(wq_rest_in, 16)
            with sp_eng.Fori(1, 4) as it:
                for j in range(2):
                    sp_eng.wait_ge(branch_done, it * 4 + 2 * j - 2)
                    sp_eng.dma_start(w_mix[:, j, :], w_mix_d[it * 2 + j, :, :]).then_inc(wmix_in[j], 16)
            sp_eng.wait_ge(branch_done, 2 * KD)
            sp_eng.dma_start(w_out[:, CC:KD, :], w_out_d[:, CC:KD, :]).then_inc(wout_in, 16)
            sp_eng.dma_start(x_in, x_d[0:P, :]).then_inc(x_loaded, 16)
            sp_eng.dma_start(b_out_bc, b_out_d.partition_broadcast(P)).then_inc(rows_in, 16)
            with sp_eng.Fori(0, PH - 1) as h:
                sp_eng.wait_ge(q_psum, h + 1)
                sp_eng.dma_start(w_q[:, PH - 1, :, :], w_q_d[:, h + 1, :, :]).then_inc(wq_in, 16)
                sp_eng.wait_ge(x1_ready, START + h + 1)
                sp_eng.dma_start(x_in, x_d[bass.ds((h + 1) * P, P), :]).then_inc(x_loaded, 16)
            sp_eng.wait_ge(wout_done, START + NB)
            sp_eng.dma_start(w_q[:, 0, :, :], w_q_d[:, 0, :, :]).then_inc(wq0_in, 16)
            for h in range(1, 4):
                sp_eng.dma_start(w_q[:, h, :, :], w_q_d[:, h, :, :]).then_inc(wq_rest_in, 16)
            sp_eng.wait_ge(x1_ready, START + NB)
            for h in range(4, 6):
                sp_eng.dma_start(w_q[:, h, :, :], w_q_d[:, h, :, :]).then_inc(wq_rest_in, 16)
            sp_eng.dma_start(ln2_g_bc, ln2_g_d.partition_broadcast(P)).then_inc(rows2_in, 16)
            sp_eng.dma_start(ln2_b_bc, ln2_b_d.partition_broadcast(P)).then_inc(rows2_in, 16)
            with sp_eng.Fori(0, NB) as b:
                sp_eng.wait_ge(out_ready, b + 1)
                sp_eng.dma_start(out_d[bass.ds(b * P, P), :], pre2).then_inc(stored, 16)
            sp_eng.wait_ge(stored, 16 * START + 16 * NB)

        @block.gpsimd
        def _(pool):
            for s in (psum_read + expert_used + mixed +
                      [pre_read, wout_done, att_done, sp_done, suffix_done, av_done, acc_done, out_read, z_done, x1_ready, q_ready,
                       qT_ready, score_ready, y_read, idx_ready, idx_copied, x1T_psum]):
                pool.sem_inc(s, START)
            pool.sem_inc(stored, 16 * START)
            pool.memset(conv_in[:, :, 0:PAD], 0.0).then_inc(pad_ready, 1)
            pool.memset(mean_w, 1.0 / CONV).then_inc(consts, 1)
            pool.memset(one_row[0:1, :], 1.0).then_inc(consts, 1)
            pool.memset(neg_ones, -1.0).then_inc(consts, 1)
            pool.memset(zeros[:, :], 0.0).then_inc(consts, 1)
            pool.memset(tri, -1.0).then_inc(pool_step, 1)
            pool.iota(iota_i[:, :], pattern=[[1, TOPK]], base=0, channel_multiplier=0).then_inc(consts, 1)
            pool.wait_ge(pool_step, 1)
            pool.affine_select(out=tri, in_=tri, compare_op=ALU.is_ge, fill=0.0, base=0,
                               pattern=[[-1, P]], channel_multiplier=1).then_inc(consts, 1)

            pool.wait_ge(var_done, 1)
            pool.memset(q_pair[DH:P, 0, :], 0.0).then_inc(q_zeroed, 1)
            pool.memset(q_pair[0:DH, 1, :], 0.0).then_inc(q_zeroed, 1)
            with pool.Fori(0, PAIRS) as p:
                order = sorted([(u, 0) for u in DIAG_NO] + [(u + 1.5, 1) for u in DIAG_NO])
                for key, what in order:
                    u = int(key) if what == 0 else int(key - 1.5)
                    Q, kb, hd = UNITS[u]
                    c0 = kb * P - Q * HALF
                    if what == 0:
                        wait_alone(pool, sp_done, START + p * NU + u + 1, consts)
                        tile, signal = sp[:, u % 3, c0:c0 + P], sp_masked
                    else:
                        wait_alone(pool, att_done, START + p * NU + u + 1, consts)
                        tile, signal = att[:, u % 3, c0:c0 + P], att_masked
                    pool.affine_select(out=tile, in_=tile, compare_op=ALU.is_gt, fill=0.0, base=0,
                                       pattern=[[1, P]], channel_multiplier=-1).then_inc(signal, 1)

            pool.memset(ident, 0.0).then_inc(pool_step, 1)
            pool.wait_ge(pool_step, 2)
            pool.affine_select(out=ident, in_=ident, compare_op=ALU.not_equal, fill=1.0, base=0,
                               pattern=[[-1, P]], channel_multiplier=1).then_inc(consts, 1)

            with pool.Fori(0, NB * PH) as t:
                wait_alone(pool, idx_ready, START + t + 1, consts)
                for s in range(TOPK):
                    if s % RING == 0:
                        pool.tensor_copy(idx_now[:, s:s + RING],
                                         idx_f[:, s:s + RING]).then_inc(idx_copied, 1)
                        wait_alone(pool, idx_copied, START + t * 2 + (s // RING + 1), consts)
                    wait_alone(pool, expert_used[s % RING], START + t * 2 + s // RING, consts)
                    pool.indirect_dma_start(
                        out=ring[:, s % RING, :], out_offset=None, in_=uv_d,
                        in_offset=bass.IndirectOffsetOnAxis(ap=idx_now[:, s:s + 1], axis=0),
                    ).then_inc(gathered[s % RING], 16)

        @block.tensor
        def _(pe):
            pe.wait_ge(consts, 6)

            with pe.Fori(0, 4) as it:
                for j in range(4):
                    pe.wait_ge(w_in[j], (it + 1) * 16)
                    pe.wait_ge(psum_read[j], START + it)
                    for k in range(KD):
                        if j == 0:
                            pe.wait_ge(xT_in[k], 16)
                        for h in range(2):
                            last = nc.tensor.matmul(ps[:, 2 * j + h, :], w_ring[:, j, k, :],
                                                    xT[:, k, h * HALF:(h + 1) * HALF],
                                                    start=(k == 0), stop=(k == KD - 1))
                    last.then_inc(proj_done, 1)
            pe.wait_ge(wv_in, 16)
            pe.wait_ge(bv_in, 16)
            for b in range(NB):
                j = b % 4
                pe.wait_ge(psum_read[j], START + b // 4 + 4)
                nc.tensor.matmul(ps[:, 2 * j, :], one_row[0:1, :], bv_row[0:1, :], start=True, stop=False)
                for k in range(KD):
                    last = nc.tensor.matmul(ps[:, 2 * j, :], xT[:, k, b * P:(b + 1) * P],
                                            w_v[:, k, :], start=False, stop=(k == KD - 1))
                last.then_inc(v_done, 1)

            pe.wait_ge(conv_done, CC)
            pe.wait_ge(psum_read[0], START + 6)
            for h in range(2):
                for c in range(CC):
                    last = nc.tensor.matmul(ps[:, h, :], mean_w, conv[:, c, h * HALF:(h + 1) * HALF],
                                            start=(c == 0), stop=(c == CC - 1))
            last.then_inc(mean_done, 1)
            pe.wait_ge(psum_read[1], START + 6)
            for c in range(CC):
                pe.wait_ge(squared, c + 1)
                for h in range(2):
                    last = nc.tensor.matmul(ps[:, 2 + h, :], mean_w, conv_sq[:, c, h * HALF:(h + 1) * HALF],
                                            start=(c == 0), stop=(c == CC - 1))
            last.then_inc(var_done, 1)

            pe.wait_ge(std_done, 1)
            pe.wait_ge(psum_read[2], START + 6)
            pe.wait_ge(psum_read[3], START + 6)

            def score_mm(p, u):
                Q, kb, hd = UNITS[u]
                c0 = max(0, kb * P - Q * HALF)
                pe.wait_ge(att_done, START + p * NU + (u - 3 if u >= 4 else 0))
                nc.tensor.matmul(ps[:, u % 4, c0:HALF], k_pair[:, kb * P:(kb + 1) * P],
                                 q_pair[:, hd, Q * HALF + c0:(Q + 1) * HALF],
                                 start=True, stop=True, skip_group_check=True).then_inc(z_done, 1)

            def suffix_mm(p, u):
                Q, kb, hd = UNITS[u]
                c0 = max(0, kb * P - Q * HALF)
                diagonal = kb >= 4 * Q
                old = c0 + P if diagonal else 0
                if diagonal:
                    pe.wait_ge(sp_masked, p * N_DIAG + DIAG_NO[u] + 1)
                else:
                    pe.wait_ge(sp_done, START + p * NU + u + 1)
                first = kb == 4 * Q + 3
                last = nc.tensor.matmul(ps[:, u % 4, c0:HALF], tri, sp[:, u % 3, c0:HALF],
                                        start=False, stop=True, skip_group_check=True)
                if not first:
                    pe.wait_ge(acc_done, START + p * N_ACC + ACC_NO[u - 2] + 1)
                    last = nc.tensor.matmul(ps[:, u % 4, old:HALF], neg_ones, acc[:, hd, (kb + 1) % 2, old:HALF],
                                            start=False, stop=True, skip_group_check=True)
                last.then_inc(suffix_done, 1)

            def value_mm(p, u):
                Q, kb, hd = UNITS[u]
                c0 = max(0, kb * P - Q * HALF)
                first = kb == 4 * Q + 3
                if kb >= 4 * Q:
                    pe.wait_ge(att_masked, p * N_DIAG + DIAG_NO[u] + 1)
                else:
                    pe.wait_ge(att_done, START + p * NU + u + 1)
                if first and hd == 0:
                    pe.wait_ge(out_read, START + p * 2)
                r = slice(hd * DH, (hd + 1) * DH)
                nc.tensor.matmul(ps[r, 4 + Q, c0:HALF], v_pair[:, kb, hd * DH:(hd + 1) * DH],
                                 att[:, u % 3, c0:HALF],
                                 start=first, stop=(kb == 0), skip_group_check=True).then_inc(av_done, 1)

            with pe.Fori(0, PAIRS) as p:
                pe.wait_ge(k_staged, p + 1)
                for u in range(3):
                    score_mm(p, u)
                pe.wait_ge(v_staged, p + 1)
                for t in range(NU + 1):
                    if t + 3 < NU:
                        score_mm(p, t + 3)
                    if t < NU:
                        suffix_mm(p, t)
                    if t >= 1:
                        value_mm(p, t - 1)

            pe.wait_ge(swish_done, CC)
            pe.wait_ge(out_read, START + PAIRS * 2)
            with pe.Fori(0, KD // 2) as i:
                for j in range(2):
                    pe.wait_ge(wmix_in[j], (i + 1) * 16)
                    for h in range(2):
                        cs = slice(h * HALF, (h + 1) * HALF)
                        pe.wait_ge(mixed[h], START + i * 2 + j)
                        for g in range(2):
                            for k in range(KD):
                                last = nc.tensor.matmul(ps[:, 4 * h + g, :],
                                                        w_mix[:, j, g * D + k * P:g * D + (k + 1) * P],
                                                        xT[:, k, cs], start=(k == 0), stop=(k == KD - 1))
                        last.then_inc(gates_done, 1)
                        for y, src in ((0, conv), (1, attT)):
                            for k in range(CC):
                                o = 2 * D + y * HALF + k * P
                                last = nc.tensor.matmul(ps[:, 4 * h + 2 + y, :], w_mix[:, j, o:o + P],
                                                        src[:, k, cs], start=(k == 0), stop=(k == CC - 1))
                        last.then_inc(branch_done, 1)

            def wout_mm(b, k0, k1):
                if k0 == 0:
                    wait_alone(pe, blk_staged, b + 1, consts)
                    pe.wait_ge(pre_read, START + b)
                for k in range(k0, k1):
                    for h in range(2):
                        last = nc.tensor.matmul(ps[:, 6 + h, :], mix_blk[:, k, :],
                                                w_out[:, k, h * HALF:(h + 1) * HALF],
                                                start=(k == 0), stop=(k == KD - 1))
                if k1 == KD:
                    last.then_inc(wout_done, 1)

            def transposes(b):
                pe.wait_ge(x1_staged, b + 1)
                for k in range(KD):
                    last = nc.tensor.transpose(ps_flat[:, k * P:(k + 1) * P], x1_blk[:, k * P:(k + 1) * P], ident)
                last.then_inc(x1T_psum, 1)

            def queries(r, place):
                pe.wait_ge(q_ready, START + r)
                for k in range(KD):
                    last = nc.tensor.matmul(ps[:, 2, 0:2 * P], x1T[:, k, :], w_q[:, place, k, :],
                                            start=(k == 0), stop=(k == KD - 1))
                last.then_inc(q_psum, 1)

            def query_transposes(r):
                pe.wait_ge(q_ready, START + r + 1)
                pe.wait_ge(qT_ready, START + r)
                for half in range(2):
                    last = nc.tensor.transpose(ps[:, 2, (2 + half) * P:(3 + half) * P],
                                               q_nat[:, half * P:(half + 1) * P], ident)
                last.then_inc(qT_psum, 1)

            def scores(r, h):
                pe.wait_ge(qT_ready, START + r + 1)
                pe.wait_ge(score_ready, START + r)
                for half in range(2):
                    last = nc.tensor.matmul(ps[:, 3, half * P:(half + 1) * P], q_sb[:, half, :],
                                            keysT[:, h, half, :], start=True, stop=True)
                last.then_inc(score_psum, 1)

            def experts(t, g):
                for s in range(2 * g, 2 * g + 2):
                    pe.wait_ge(diag_ready, t * TOPK + s + 1)
                    for h in range(2):
                        last = nc.tensor.matmul(ps[:, 4 + h, :], diag[:, s % DIAGS, :],
                                                ring[:, s % RING, D + h * HALF:D + (h + 1) * HALF],
                                                start=False, stop=False, skip_group_check=True)
                    last.then_inc(expert_used[s % RING], 1)

            def clear_y(b):
                pe.wait_ge(y_read, START + b)
                for h in range(2):
                    nc.tensor.matmul(ps[:, 4 + h, :], zeros[:, 0:P], zeros[:, :], start=True, stop=True,
                                     skip_group_check=True)

            def experts_and_retrieval(t, r, h, place, b5=None):
                for g in range(TOPK // 2):
                    if r is not None and g == 0:
                        queries(r, place)
                    if r is not None and g == 1:
                        query_transposes(r)
                    if r is not None and g == 2:
                        scores(r, h)
                    if b5 is not None and 1 <= g <= 4:
                        wout_mm(b5, 2 * g - 2, 2 * g)
                    experts(t, g)

            for h in range(2):
                pe.wait_ge(mixed[h], START + KD)
            pe.wait_ge(wout_in, 16)
            wout_mm(0, 0, CC)
            pe.wait_ge(wout_in, 32)
            wout_mm(0, CC, KD)
            pe.wait_ge(consts, 7)
            pe.wait_ge(keys_in, 16)
            pe.wait_ge(wq_in, 16)
            transposes(0)
            pe.wait_ge(x1T_ready, 1)
            queries(0, PH - 1)
            query_transposes(0)
            scores(0, 0)
            clear_y(0)
            with pe.Fori(0, PH - 1) as h:
                wait_alone(pe, wq_in, 16 * h + 32, consts)
                experts_and_retrieval(h, h + 1, h + 1, PH - 1, h + 1)
            transposes(1)
            pe.wait_ge(x1T_ready, 2)
            pe.wait_ge(wq0_in, 16)
            experts_and_retrieval(PH - 1, PH, 0, 0)
            pe.wait_ge(wq_rest_in, 16 * (PH - 2))
            with pe.Fori(1, NB - 1) as b:
                clear_y(b)
                with pe.Fori(0, PH - 1) as h:
                    experts_and_retrieval(b * PH + h, b * PH + h + 1, h + 1, h + 1)
                transposes(b + 1)
                wait_alone(pe, x1T_ready, b + 2, consts)
                experts_and_retrieval(b * PH + (PH - 1), b * PH + PH, 0, 0)
            clear_y(NB - 1)
            with pe.Fori(0, PH - 1) as h:
                experts_and_retrieval(h + (NB - 1) * PH, h + ((NB - 1) * PH + 1), h + 1, h + 1)
            experts_and_retrieval(NB * PH - 1, None, None, None)

        @block.scalar
        def _(act):
            act.wait_ge(cols_in, 16)
            act.wait_ge(eps_ready, 1)
            nc.scalar.mul(q_bias8[:, :], cols[:, C_Q:C_Q + CC], DH ** -0.5).then_inc(qb_ready, 1)
            with act.Fori(0, 2) as it:
                for j in (1, 3):
                    act.wait_ge(proj_done, it * 4 + j + 1)
                    act.wait_ge(psum_read[j - 1], START + it)
                    nc.scalar.activation(glu_gate[:, j // 2, :], ps_flat[:, j * 2 * HALF:(j + 1) * 2 * HALF],
                                         ACT.Sigmoid, bias=cols[:, bass.ds(it * 2 + (C_G + j // 2), 1)]
                                         ).then_inc(psum_read[j], 1)
            act.wait_ge(qb_ready, 1)
            for j in range(4):
                act.wait_ge(proj_done, 8 + j + 1)
                nc.scalar.activation(qT[:, j, :], ps_flat[:, j * 2 * HALF:(j + 1) * 2 * HALF], ACT.Identity,
                                     bias=q_bias8[:, j:j + 1], scale=DH ** -0.5).then_inc(psum_read[j], 1)
            for j in range(4):
                act.wait_ge(proj_done, 12 + j + 1)
                nc.scalar.activation(kT[:, j, :], ps_flat[:, j * 2 * HALF:(j + 1) * 2 * HALF], ACT.Identity,
                                     bias=cols[:, C_K + j:C_K + j + 1]).then_inc(psum_read[j], 1)
            with act.Fori(0, 2) as tt:
                for j in range(4):
                    act.wait_ge(v_done, tt * 4 + j + 1)
                    nc.scalar.activation(v_sb[:, tt * 4 + j, :], ps[:, 2 * j, :], ACT.Copy).then_inc(psum_read[j], 1)

            for c in range(CC):
                act.wait_ge(centred, c + 1)
                nc.scalar.activation(conv_sq[:, c, :], conv[:, c, :], ACT.Square).then_inc(squared, 1)
            act.wait_ge(var_done, 1)
            nc.scalar.activation(rstd_row, ps_flat[:, 2 * HALF:4 * HALF], ACT.Sqrt,
                                 bias=eps_col[:, :]).then_inc(std_done, 1)
            for c in range(CC):
                act.wait_ge(normed, c + 1)
                nc.scalar.activation(conv[:, c, :], conv[:, c, :], ACT.Silu, bias=cols[:, C_LB + c:C_LB + c + 1],
                                     scale=cols[:, C_LG + c:C_LG + c + 1]).then_inc(swish_done, 1)

            def soft_log(p, u):
                Q, kb, hd = UNITS[u]
                c0 = max(0, kb * P - Q * HALF)
                act.wait_ge(z_done, START + p * NU + u + 1)
                act.wait_ge(sp_done, START + p * NU + (u - 3 if u >= 4 else 0))
                nc.scalar.activation(el[:, u % 4, c0:HALF], ps[:, u % 4, c0:HALF], ACT.Abs).then_inc(abs_done, 1)
                act.wait_ge(abs_done, p * NU + u + 1)
                nc.scalar.activation(el[:, u % 4, c0:HALF], el[:, u % 4, c0:HALF], ACT.Exp, scale=-1.0).then_inc(e_done, 1)
                act.wait_ge(e_done, p * NU + u + 1)
                nc.scalar.activation(el[:, u % 4, c0:HALF], el[:, u % 4, c0:HALF], ACT.Ln, bias=1.0).then_inc(l_done, 1)

            def weights(p, u):
                Q, kb, hd = UNITS[u]
                c0 = max(0, kb * P - Q * HALF)
                act.wait_ge(suffix_done, START + p * NU + u + 1)
                act.wait_ge(av_done, START + p * NU + (u - 2 if u >= 3 else 0))
                nc.scalar.activation(att[:, u % 3, c0:HALF], ps[:, u % 4, c0:HALF], ACT.Exp).then_inc(att_done, 1)

            def evacuate(p, Q, last_unit):
                act.wait_ge(av_done, START + p * NU + last_unit + 1)
                nc.scalar.activation(attT[:, p, Q * HALF:(Q + 1) * HALF], ps[:, 4 + Q, :], ACT.Copy).then_inc(out_read, 1)

            act.preload_act_table_set("natural_log_exp_and_others")
            with act.Fori(0, PAIRS) as p:
                soft_log(p, 0)
                soft_log(p, 1)
                for t in range(NU):
                    if t + 2 < NU:
                        soft_log(p, t + 2)
                    weights(p, t)
                    if t == 10:
                        evacuate(p, 0, 7)
                evacuate(p, 1, NU - 1)

            with act.Fori(0, KD) as m:
                for h in range(2):
                    act.wait_ge(mixed[h], START + m)
                    wait_alone(act, gates_done, m * 2 + h + 1, cols_in)
                    for g in range(2):
                        nc.scalar.activation(gate_tmp[:, h, g, :], ps[:, 4 * h + g, :], ACT.Sigmoid,
                                             bias=cols[:, bass.ds(m + (C_GA + g * KD), 1)]).then_inc(sigs_ready, 1)
            def stage_mix(b):
                wait_alone(act, wout_done, START + b, cols_in)
                nc.scalar.activation(mix_blk.rearrange("p a b -> p (a b)"), x1[:, b, :],
                                     ACT.Copy).then_inc(blk_staged, 1)

            def std1(b):
                act.wait_ge(var1_ready, b + 1)
                nc.scalar.activation(std[:, :], mv[:, 1:2], ACT.Sqrt, bias=eps_col[:, :]).then_inc(std1_ready, 1)

            def x1_stage(b):
                act.wait_ge(x1T_psum, START + b)
                nc.scalar.activation(x1_blk, x1[:, b, :], ACT.Copy).then_inc(x1_staged, 1)

            def x1T_out(b):
                act.wait_ge(x1T_psum, START + b + 1)
                nc.scalar.activation(x1T.rearrange("p a b -> p (a b)"), ps_flat[:, 0:D], ACT.Copy).then_inc(x1T_ready, 1)

            def q_out(r):
                act.wait_ge(q_psum, r + 1)
                nc.scalar.activation(q_nat, ps[:, 2, 0:2 * P], ACT.Copy).then_inc(q_ready, 1)

            def qT_out(r):
                act.wait_ge(qT_psum, r + 1)
                nc.scalar.activation(q_sb.rearrange("p a b -> p (a b)"), ps[:, 2, 2 * P:4 * P], ACT.Copy).then_inc(qT_ready, 1)

            def score_out(r):
                act.wait_ge(score_psum, r + 1)
                act.wait_ge(idx_ready, START + r)
                nc.scalar.activation(score.rearrange("p a b -> p (a b)"), ps[:, 3, 0:2 * NKEY],
                                     ACT.Copy).then_inc(score_ready, 1)

            def soft_exp(r):
                act.wait_ge(shifted, r + 1)
                nc.scalar.activation(soft, soft, ACT.Exp, accum_out=den[:, :]).then_inc(exp_ready, 1)

            def expert_weights(t, g, steps):
                act.wait_ge(dots_done, t * (TOPK // 2) + g + 1)
                s0 = 2 * g
                steps.link(nc.scalar.activation(gcol[:, s0:s0 + 2], hcol[:, s0:s0 + 2], ACT.Gelu))
                for s in (s0, s0 + 1):
                    last = nc.scalar.activation(wcol[:, s:s + 1], gcol[:, s:s + 1], ACT.Copy,
                                                scale=gates_flat[:, bass.ds(t * TOPK + s, 1)])
                steps.link(last)
                for s in (s0, s0 + 1):
                    f = s - DIAGS
                    act.wait_ge(expert_used[f % RING], START + t * 2 + (f // RING + 1 if f >= 0 else 0))
                    nc.scalar.activation(diag[:, s % DIAGS, :], ident, ACT.Copy,
                                         scale=wcol[:, s:s + 1]).then_inc(diag_ready, 1)

            def finish_std(b):
                act.wait_ge(var2_ready, b + 1)
                nc.scalar.activation(std[:, :], mv[:, 1:2], ACT.Sqrt, bias=eps_col[:, :]).then_inc(std2_ready, 1)

            def experts_and_retrieval(t, r, b5=None):
                steps = Steps(act, gelu_step, t * TOPK)
                if b5 is not None:
                    stage_mix(b5)
                for g in range(TOPK // 2):
                    if r is not None and g == 7:
                        soft_exp(r)
                    expert_weights(t, g, steps)
                    if r is not None and g == 0:
                        q_out(r)
                    if r is not None and g == 1:
                        qT_out(r)
                        score_out(r)
                assert steps.n == TOPK
                if b5 is not None:
                    std1(b5)

            act.wait_ge(consts, 7)
            for h in range(2):
                act.wait_ge(mixed[h], START + KD)
            stage_mix(0)
            std1(0)
            act.wait_ge(x1_ready, START + 1)
            x1_stage(0)
            x1T_out(0)
            q_out(0)
            qT_out(0)
            score_out(0)
            soft_exp(0)
            with act.Fori(0, PH - 1) as h:
                act.wait_ge(gates_ready, h + 1)
                experts_and_retrieval(h, h + 1, h + 1)
            act.wait_ge(x1_ready, START + NB)
            x1_stage(1)
            x1T_out(1)
            act.wait_ge(gates_ready, PH)
            experts_and_retrieval(PH - 1, PH)
            finish_std(0)
            with act.Fori(1, NB - 1) as b:
                with act.Fori(0, PH - 1) as h:
                    act.wait_ge(gates_ready, b * PH + h + 1)
                    experts_and_retrieval(b * PH + h, b * PH + h + 1)
                x1_stage(b + 1)
                x1T_out(b + 1)
                act.wait_ge(gates_ready, b * PH + PH)
                experts_and_retrieval(b * PH + (PH - 1), b * PH + PH)
                finish_std(b)
            with act.Fori(0, PH - 1) as h:
                act.wait_ge(gates_ready, h + ((NB - 1) * PH + 1))
                experts_and_retrieval(h + (NB - 1) * PH, h + ((NB - 1) * PH + 1))
            act.wait_ge(gates_ready, NB * PH)
            experts_and_retrieval(NB * PH - 1, None)
            finish_std(NB - 1)

        @block.vector
        def _(dve):
            nc.vector.memset(eps_col[:, :], EPS).then_inc(eps_ready, 1)
            dve.wait_ge(cols_in, 16)
            dve.wait_ge(pad_ready, 1)
            with dve.Fori(0, 2) as it:
                for j in (0, 2):
                    dve.wait_ge(proj_done, it * 4 + j + 1)
                    dve.wait_ge(psum_read[j + 1], START + it + 1)
                    nc.vector.scalar_tensor_tensor(
                        out=conv_in[:, it * 2 + j // 2, PAD:PAD + S], in0=ps_flat[:, j * 2 * HALF:(j + 1) * 2 * HALF],
                        scalar=cols[:, bass.ds(it * 2 + (C_A + j // 2), 1)], in1=glu_gate[:, j // 2, :],
                        op0=ALU.add, op1=ALU.mult).then_inc(psum_read[j], 1)
            dve.wait_ge(psum_read[0], START + 2)
            dve.wait_ge(psum_read[2], START + 2)
            with dve.Fori(0, CC) as c:
                steps = Steps(dve, conv_step, c * PAD)
                steps.link(nc.vector.tensor_scalar(conv[:, c, :], conv_in[:, c, 0:S],
                                                   cols[:, bass.ds(c * TAPS + C_CW, 1)],
                                                   cols[:, bass.ds(c + C_CB, 1)], ALU.mult, ALU.add))
                for k in range(1, TAPS):
                    ins = nc.vector.scalar_tensor_tensor(
                        out=conv[:, c, :], in0=conv_in[:, c, k:k + S], scalar=cols[:, bass.ds(c * TAPS + (C_CW + k), 1)],
                        in1=conv[:, c, :], op0=ALU.mult, op1=ALU.add)
                    if k < TAPS - 1:
                        steps.link(ins)
                ins.then_inc(conv_done, 1)
                assert steps.n == PAD
            dve.wait_ge(conv_done, CC)
            dve.wait_ge(mean_done, 1)
            for c in range(CC):
                nc.vector.tensor_tensor(conv[:, c, :], conv[:, c, :], ps_flat[:, 0:2 * HALF],
                                        ALU.subtract).then_inc(centred, 1)
            dve.wait_ge(std_done, 1)
            nc.vector.reciprocal(rstd_row, rstd_row).then_inc(rstd_done, 1)
            dve.wait_ge(rstd_done, 1)
            dve.wait_ge(centred, CC)
            for c in range(CC):
                nc.vector.tensor_tensor(conv[:, c, :], conv[:, c, :], rstd_row, ALU.mult).then_inc(normed, 1)
            dve.wait_ge(normed, CC)

            def softplus(p, u):
                Q, kb, hd = UNITS[u]
                c0 = max(0, kb * P - Q * HALF)
                dve.wait_ge(l_done, p * NU + u + 1)
                dve.wait_ge(suffix_done, START + p * NU + (u - 2 if u >= 3 else 0))
                dve.wait_ge(acc_done, START + p * N_ACC + (sum(v <= u - 3 for v in ACC_NO) if u >= 3 else 0))
                nc.vector.scalar_tensor_tensor(out=sp[:, u % 3, c0:HALF], in0=ps[:, u % 4, c0:HALF], scalar=0.0,
                                               in1=el[:, u % 4, c0:HALF], op0=ALU.max, op1=ALU.add).then_inc(sp_done, 1)

            def accumulate(p, u):
                Q, kb, hd = UNITS[u]
                if kb == 0:
                    return
                c0 = max(0, kb * P - Q * HALF)
                diagonal = kb >= 4 * Q
                old = c0 + P if diagonal else 0
                first = kb == 4 * Q + 3
                if diagonal:
                    dve.wait_ge(sp_masked, p * N_DIAG + DIAG_NO[u] + 1)
                    ins = nc.vector.tensor_copy(acc[:, hd, kb % 2, c0:old], sp[:, u % 3, c0:old])
                else:
                    dve.wait_ge(sp_done, START + p * NU + u + 1)
                if not first:
                    dve.wait_ge(acc_done, START + p * N_ACC + ACC_NO[u - 2] + 1)
                    ins = nc.vector.tensor_tensor(acc[:, hd, kb % 2, old:HALF], acc[:, hd, (kb + 1) % 2, old:HALF],
                                                  sp[:, u % 3, old:HALF], ALU.add)
                ins.then_inc(acc_done, 1)

            dve.wait_ge(psum_read[3], START + 6)
            dve.wait_ge(q_zeroed, 2)
            with dve.Fori(0, PAIRS) as p:
                dve.wait_ge(z_done, START + p * NU)
                nc.vector.tensor_copy(k_pair, kT[:, p, :])
                for hd in range(2):
                    r = slice(hd * DH, (hd + 1) * DH)
                    last = nc.vector.tensor_copy(q_pair[r, hd, :], qT[r, p, :])
                last.then_inc(k_staged, 1)
                dve.wait_ge(av_done, START + p * NU)
                nc.vector.tensor_copy(v_pair, v_sb[:, :, bass.ds(p * P, P)]).then_inc(v_staged, 1)
                softplus(p, 0)
                for t in range(NU):
                    if t + 1 < NU:
                        softplus(p, t + 1)
                    accumulate(p, t)

            with dve.Fori(0, KD) as m:
                for h in range(2):
                    dve.wait_ge(sigs_ready, m * 4 + 2 * h + 2)
                    dve.wait_ge(branch_done, m * 2 + h + 1)
                    nc.vector.scalar_tensor_tensor(out=gate_tmp[:, h, 0, :], in0=ps[:, 4 * h + 2, :],
                                                   scalar=cols[:, bass.ds(m + C_PW, 1)], in1=gate_tmp[:, h, 0, :],
                                                   op0=ALU.add, op1=ALU.mult)
                    nc.vector.tensor_tensor(gate_tmp[:, h, 1, :], ps[:, 4 * h + 3, :], gate_tmp[:, h, 1, :],
                                            ALU.mult).then_inc(mix_step, 1)
                    dve.wait_ge(mix_step, m * 2 + h + 1)
                    nc.vector.tensor_tensor(mixT[:, h * CC:(h + 1) * CC, m, :],
                                            gate_tmp[:, h, 0, :].rearrange("p (b t) -> p b t", t=P),
                                            gate_tmp[:, h, 1, :].rearrange("p (b t) -> p b t", t=P),
                                            ALU.add).then_inc(mixed[h], 1)

            def layer_norm(tile, steps, var_ready, std_ready, turn, g_bc, b_bc, out):
                for h in range(2):
                    last = nc.vector.bn_stats(stats[:, h, :], tile[:, h * HALF:(h + 1) * HALF])
                steps.link(last)
                nc.vector.bn_aggr(mv[:, :], stats[:, :, :].rearrange("p a b -> p (a b)")).then_inc(var_ready, 1)
                dve.wait_ge(std_ready, turn + 1)
                steps.link(nc.vector.reciprocal(rstd[:, :], std[:, :]))
                steps.link(nc.vector.tensor_scalar(tile, tile, mv[:, 0:1], rstd[:, 0:1], ALU.subtract, ALU.mult))
                steps.link(nc.vector.tensor_tensor(tile, tile, g_bc, ALU.mult))
                return nc.vector.tensor_tensor(out, tile, b_bc, ALU.add)

            def x1_block(b):
                steps = Steps(dve, ln1_step, b * 5, consts)
                dve.wait_ge(wout_done, START + b + 1)
                dve.wait_ge(x_loaded, (b + 1) * 16)
                nc.vector.scalar_tensor_tensor(out=x_in, in0=x_in, scalar=ALPHA, in1=ps_flat[:, 6 * HALF:8 * HALF],
                                               op0=ALU.mult, op1=ALU.add).then_inc(pre_read, 1)
                dve.wait_ge(pre_read, START + b + 1)
                steps.link(nc.vector.tensor_tensor(x_in, x_in, b_out_bc, ALU.add))
                layer_norm(x_in, steps, var1_ready, std1_ready, b, ln1_g_bc, ln1_b_bc,
                           x1[:, b, :]).then_inc(x1_ready, 1)
                assert steps.n == 5

            dve.wait_ge(consts, 6)
            nc.vector.tensor_copy(iota16[:, :], iota_i[:, :]).then_inc(iota_ready, 1)
            dve.wait_ge(iota_ready, 1)

            def topk_half(steps, half):
                s_half = score[:, half, :]
                steps.link(nc.vector.max(top_v[:, half, 0:8], s_half))
                steps.link(nc.vector.max_index(top_i[:, half, 0:8], top_v[:, half, 0:8], s_half))
                steps.link(nc.vector.match_replace(s_half, top_v[:, half, 0:8], s_half, NEG))
                steps.link(nc.vector.max(top_v[:, half, 8:16], s_half))
                steps.link(nc.vector.max_index(top_i[:, half, 8:16], top_v[:, half, 8:16], s_half))

            def topk_pairs(steps, r):
                steps.link(nc.vector.tensor_tensor(cand, top_v[:, 0, :].unsqueeze(2).to_broadcast([P, TOPK, TOPK]),
                                                   top_v[:, 1, :].unsqueeze(1).to_broadcast([P, TOPK, TOPK]), ALU.add))
                cf = cand.rearrange("p a b -> p (a b)")
                g0, g1 = top_s[:, 0:8], top_s[:, 8:16]
                steps.link(nc.vector.max(g0, cf))
                steps.link(nc.vector.max_index(pos[:, 0:8], g0, cf))
                steps.link(nc.vector.match_replace(cf, g0, cf, NEG))
                steps.link(nc.vector.max(g1, cf))
                steps.link(nc.vector.max_index(pos[:, 8:16], g1, cf))
                nc.vector.tensor_scalar(soft, top_s[:, :], top_s[:, 0:1], None, ALU.subtract).then_inc(shifted, 1)

            def expert_index(steps, r):
                nc.vector.tensor_scalar(top_i[:, 0, :], top_i[:, 0, :], 7, None, ALU.logical_shift_left)
                nc.vector.tensor_scalar(pos_ab[:, :, 0], pos[:, :], 4, None, ALU.logical_shift_right)
                steps.link(nc.vector.tensor_scalar(pos_ab[:, :, 1], pos[:, :], 15, None, ALU.bitwise_and))
                oh = onehot.rearrange("p k (a j) -> p k a j", a=2)
                steps.link(nc.vector.tensor_tensor(
                    oh, pos_ab[:, :, :].unsqueeze(3).to_broadcast([P, TOPK, 2, TOPK]),
                    iota16[:, :].unsqueeze(1).unsqueeze(1).to_broadcast([P, TOPK, 2, TOPK]), ALU.is_equal))
                steps.link(nc.vector.tensor_tensor(
                    oh, oh, top_i[:, :, :].unsqueeze(1).to_broadcast([P, TOPK, 2, TOPK]), ALU.mult))
                wait_alone(dve, idx_copied, START + r * 2, consts)
                nc.vector.tensor_reduce(idx_f, onehot, AX_X, ALU.add).then_inc(idx_ready, 1)

            def softmax(r):
                dve.wait_ge(exp_ready, r + 1)
                nc.vector.reciprocal(rden[:, :], den[:, :]).then_inc(soft_step, 1)
                dve.wait_ge(soft_step, r + 1)
                nc.vector.tensor_scalar(gates_flat[:, bass.ds(r * TOPK, TOPK)], soft, rden[:, 0:1], None,
                                        ALU.mult).then_inc(gates_ready, 1)

            def dots(b, t, g):
                for s in range(2 * g, 2 * g + 2):
                    dve.wait_ge(gathered[s % RING], (t * 2 + (s // RING + 1)) * 16)
                    last = nc.vector.scalar_tensor_tensor(
                        out=ring[:, s % RING, 0:D], in0=x1[:, b, :], scalar=1.0, in1=ring[:, s % RING, 0:D],
                        op0=ALU.mult, op1=ALU.mult, accum_out=hcol[:, s:s + 1])
                last.then_inc(dots_done, 1)

            def finish(b):
                steps = Steps(dve, ln2_step, b * 4, consts)
                dve.wait_ge(expert_used[RING - 1], START + b * 2 * PH + 2 * PH)
                dve.wait_ge(expert_used[RING - 2], START + b * 2 * PH + 2 * PH)
                dve.wait_ge(stored, 16 * START + b * 16)
                nc.vector.scalar_tensor_tensor(out=pre2, in0=x1[:, b, :], scalar=ALPHA,
                                               in1=ps_flat[:, 4 * HALF:6 * HALF],
                                               op0=ALU.mult, op1=ALU.add).then_inc(y_read, 1)
                dve.wait_ge(y_read, START + b + 1)
                layer_norm(pre2, steps, var2_ready, std2_ready, b, ln2_g_bc, ln2_b_bc, pre2).then_inc(out_ready, 1)
                assert steps.n == 4

            def experts_and_retrieval(b, t, r, b5=None):
                steps = Steps(dve, topk_step, r * TOPK_STEPS, consts)
                for g in range(TOPK // 2):
                    dots(b, t, g)
                    if g == 2:
                        wait_alone(dve, score_ready, START + r + 1, consts)
                        topk_half(steps, 0)
                    if g == 3:
                        topk_half(steps, 1)
                    if g == 4:
                        topk_pairs(steps, r)
                    if g == 5:
                        expert_index(steps, r)
                softmax(r)
                assert steps.n == TOPK_STEPS
                if b5 is not None:
                    x1_block(b5)

            dve.wait_ge(rows_in, 48)
            x1_block(0)
            dve.wait_ge(x1_ready, START + 1)
            steps = Steps(dve, topk_step)
            dve.wait_ge(score_ready, START + 1)
            topk_half(steps, 0)
            topk_half(steps, 1)
            topk_pairs(steps, 0)
            expert_index(steps, 0)
            assert steps.n == TOPK_STEPS, steps.n
            softmax(0)
            with dve.Fori(0, PH - 1) as h:
                experts_and_retrieval(0, h, h + 1, h + 1)
            dve.wait_ge(x1_ready, START + NB)
            experts_and_retrieval(0, PH - 1, PH)
            dve.wait_ge(rows2_in, 32)
            finish(0)
            with dve.Fori(1, NB - 1) as b:
                with dve.Fori(0, PH) as h:
                    experts_and_retrieval(b, b * PH + h, b * PH + h + 1)
                finish(b)
            with dve.Fori(0, PH - 1) as h:
                experts_and_retrieval(NB - 1, h + (NB - 1) * PH, h + ((NB - 1) * PH + 1))
            for g in range(TOPK // 2):
                dots(NB - 1, NB * PH - 1, g)
            finish(NB - 1)


def kernel(x, w_in, b_in, conv_w_dw, conv_b_dw, conv_ln_g, conv_ln_b, conv_w_pw2, conv_b_pw2, sb_w_o,
           w_out, b_out, ln1_g, ln1_b, peer_w_q, peer_keys_1, peer_keys_2, peer_u, peer_v, ln2_g, ln2_b):
    import numpy as np
    import concourse.bacc as bacc
    from concourse.bass_utils import run_bass_kernel_spmd

    def arr(a):
        return np.asarray(a)[0]

    x2, wi, bi = arr(x), arr(w_in), arr(b_in)
    col_q, col_k, col_v, col_g = 1024, 1536, 2048, 2560

    def ktile(w):
        return w.reshape(w.shape[0] // P, P, w.shape[1]).transpose(1, 0, 2)

    def slab(w, c):
        return ktile(w[:, c:c + P]).reshape(P, w.shape[0])

    def col(v):
        return v.reshape(-1, P).T

    order = []
    for c in range(CC):
        order += [c * P, CONV + c * P]
    order += [col_q + c * P for c in range(CC)] + [col_k + c * P for c in range(CC)]
    taps = arr(conv_w_dw).T.reshape(CC, P, TAPS).transpose(1, 0, 2).reshape(P, CC * TAPS)
    data = {
        "xT": ktile(x2.T),
        "x": x2,
        "w_proj": np.stack([slab(wi, c) for c in order]),
        "w_v": ktile(wi[:, col_v:col_g]),
        "w_mix": np.stack([np.concatenate([slab(wi, col_g + m * P), slab(wi, col_g + D + m * P),
                                           slab(arr(conv_w_pw2), m * P), slab(arr(sb_w_o), m * P)], axis=1)
                           for m in range(KD)]),
        "w_out": ktile(arr(w_out)),
        "w_q": ktile(arr(peer_w_q)).reshape(P, KD, PH, 2 * P).transpose(0, 2, 1, 3),
        "keys": np.stack([arr(peer_keys_1), arr(peer_keys_2)], axis=1).transpose(3, 0, 1, 2).reshape(P, PH * 2 * NKEY),
        "uv": np.concatenate([arr(peer_u), arr(peer_v)], axis=1),
        "cols": np.concatenate([col(bi[0:col_v]), col(bi[col_g:]), col(arr(conv_b_pw2)), col(arr(conv_b_dw)),
                                col(arr(conv_ln_g)), col(arr(conv_ln_b)), taps], axis=1),
        "bv": bi[col_v:col_g].reshape(1, -1),
        "b_out": arr(b_out), "ln1_g": arr(ln1_g), "ln1_b": arr(ln1_b), "ln2_g": arr(ln2_g), "ln2_b": arr(ln2_b),
    }
    nc = bacc.Bacc("TRN2", target_bir_lowering=False, num_devices=1)
    arrays, aps = {}, []
    for name, a in data.items():
        a = np.ascontiguousarray(a)
        arrays[f"{name}_dram"] = a
        aps.append(nc.dram_tensor(f"{name}_dram", a.shape, mybir.dt.from_np(a.dtype), kind="ExternalInput").ap())
    out = nc.dram_tensor("out_dram", (S, D), F32, kind="ExternalOutput").ap()
    build(nc, *aps, out)
    r = run_bass_kernel_spmd(nc, [arrays], core_ids=[0])
    return r.results[0]["out_dram"].reshape(1, S, D)
```

```python
import math
from contextlib import ExitStack

import concourse.bass as bass
from concourse import mybir

F32 = mybir.dt.float32
F32R = mybir.dt.float32r
BF16 = mybir.dt.bfloat16
U32 = mybir.dt.uint32
ALU = mybir.AluOpType
ACT = mybir.ActivationFunctionType
AX_X = mybir.AxisListType.X

P = 128
D = 1024
S = 1024
KD = D // P
NB = S // P
HALF = 512
CONV = 512
CC = CONV // P
TAPS = 31
PAD = TAPS - 1
HEADS = 8
DH = 64
PAIRS = HEADS // 2
PH = 8
NKEY = 128
TOPK = 16
NEG = -3.0e38
EPS = 1e-5
ALPHA = 2.0 ** 0.25
RING = 8
DIAGS = 4
START = 1
KB = 256

C_A, C_G, C_Q, C_K = 0, CC, 2 * CC, 3 * CC
C_GA, C_GB, C_PW = 4 * CC, 4 * CC + KD, 4 * CC + 2 * KD
C_CB = 4 * CC + 3 * KD
C_LG, C_LB = C_CB + CC, C_CB + 2 * CC
C_CW = C_CB + 3 * CC
N_COLS = C_CW + CC * TAPS


class Steps:

    def __init__(self, eng, sem, base=0, started=None):
        self.eng, self.sem, self.base, self.n, self.started = eng, sem, base, 0, started

    def link(self, ins):
        ins.then_inc(self.sem, 1)
        self.n += 1
        if self.started is None:
            self.eng.wait_ge(self.sem, self.base + self.n)
        else:
            wait_alone(self.eng, self.sem, self.base + self.n, self.started)


def wait_alone(eng, sem, value, started):
    value = eng.to_reg(value)
    eng.wait_ge(started, 1)
    eng.wait_ge(sem, value)


def attention_units():
    return [(Q, kb, hd) for Q in range(S // HALF) for kb in range(4 * Q + 3, -1, -1) for hd in range(2)]


UNITS = attention_units()
NU = len(UNITS)
DIAG_NO = {u: n for n, u in enumerate(u for u, (Q, kb, _) in enumerate(UNITS) if kb >= 4 * Q)}
ACC_NO = {u: n for n, u in enumerate(u for u, (Q, kb, _) in enumerate(UNITS) if kb > 0)}
N_DIAG, N_ACC = len(DIAG_NO), len(ACC_NO)
Z_BANKS = 6
VALUE_LAG = 2
Z_AHEAD = 4


def z_bank(u):
    return (0, 1, 2, 3, 6, 7)[u % Z_BANKS]


def build(nc, xT_d, x_d, w_proj_d, w_v_d, w_mix_d, w_out_d, w_q_d, keys_d, uv_d, cols_d, bv_d,
          b_out_d, ln1_g_d, ln1_b_d, ln2_g_d, ln2_b_d, out_d):
    ctx = ExitStack()
    with ctx:
        def sem(name):
            return ctx.enter_context(nc.semaphore(name))

        LOW, HIGH = 128, 205

        def overlay(name, first, last, dt):
            with ExitStack() as below:
                if first:
                    below.enter_context(nc.sbuf_tensor(name + "_below", [P, first * KB], F32))
                return below.enter_context(nc.sbuf_tensor(name, [P, (last - first) * KB], dt))

        arena_low = overlay("arena_low", 0, LOW, F32)
        arena_high = overlay("arena_high", LOW, HIGH, F32)
        x_hi_bytes = overlay("x_hi_bytes", 64, 96, F32R)
        w_bytes = overlay("w_bytes", 112, 160, F32R)
        w1_hi_bytes = overlay("w1_hi_bytes", 4, 20, F32R)
        x_lo_bytes = overlay("x_lo_bytes", 160, 192, F32R)
        ctx.enter_context(nc.sbuf_tensor("arenas", [P, HIGH * KB], F32))

        def at(kib, *shape):
            n = math.prod(shape)
            arena, first = (arena_low, 0) if kib < LOW else (arena_high, LOW)
            flat = arena[:, int((kib - first) * KB):int((kib - first) * KB) + n]
            if len(shape) == 1:
                return flat
            if len(shape) == 2:
                return flat.rearrange("p (a b) -> p a b", b=shape[1])
            return flat.rearrange("p (a b c) -> p a b c", b=shape[1], c=shape[2])

        xT = at(160, KD, S)
        mixT = at(0, NB, KD, P)
        x1 = at(0, NB, D)
        qT = at(32, PAIRS, S)
        kT = at(48, PAIRS, S)
        v_sb = at(128, NB, HALF)
        gate_tmp = at(48, 2, 2, HALF)
        w_v = at(112, KD, HALF)
        attT = qT
        conv = at(96, CC, S)
        conv_in = at(20, S + PAD)
        conv_sq = at(4, CC, S)
        k_pair = at(112, S)
        q_pair = at(120, 2, S)
        v_pair = at(116, NB, P)
        w_ring = at(128, 4, KD, P)
        w_mix = at(128, 2, 4 * D)[:, :, 0:3 * D]
        x_hi_r = x_hi_bytes[:, :].rearrange("p (a b) -> p a b", b=S)
        x_lo_r = x_lo_bytes[:, :].rearrange("p (a b) -> p a b", b=S)
        w_hi_r = w_bytes[:, 0:4 * D].rearrange("p (a b) -> p a b", b=2 * D)
        w_lo_r = w_bytes[:, 4 * D:12 * D].rearrange("p (a b) -> p a b", b=4 * D)
        w1_hi_r = w1_hi_bytes[:, :].rearrange("p (j a b) -> p j a b", a=KD, b=P)
        w1_lo_r = w_bytes[:, 4 * D:8 * D].rearrange("p (j a b) -> p j a b", a=KD, b=P)
        wv_lo_r = w_bytes[:, 0:4 * D].rearrange("p (a b) -> p a b", b=HALF)
        wv_hi_r = w_bytes[:, 8 * D:12 * D].rearrange("p (a b) -> p a b", b=HALF)

        def split_products(out, w_pair, x_pair, first, last):
            (w_hi, w_lo), (x_hi, x_lo) = w_pair, x_pair
            nc.tensor.matmul(out, w_hi, x_hi, start=first, stop=False)
            nc.tensor.matmul(out, w_hi, x_lo, start=False, stop=False)
            return nc.tensor.matmul(out, w_lo, x_hi, start=False, stop=last)

        glu_gate = at(0, S)
        rstd_row = at(192, S)
        el = at(0, 4, HALF)
        sp = at(8, 3, HALF)
        att = at(14, 3, HALF)
        acc = at(20, 2, 2, HALF)
        mean_w = at(28, P)
        bv_row = at(28.5, HALF)
        one_row = at(30.5, P)
        tri = at(31, P)
        neg_ones = at(31.5, P)
        w_out = at(64, KD, D)
        b_out_bc = at(96, D)
        mix_blk = at(100, KD, P)
        x_in = at(104, D)
        ln1_g_bc = at(36, D)
        ln1_b_bc = at(40, D)
        keysT = at(197, PH, 2, NKEY)
        x1T = at(32, KD, P)
        ln2_g_bc = at(36, D)
        ln2_b_bc = at(40, D)
        pre2 = at(44, D)
        q_sb = at(48, 2, P)
        score = at(49, 2, NKEY)
        cand = at(50, TOPK, TOPK)
        onehot = at(51, TOPK, 2 * TOPK)
        x1_blk = at(53, D)
        q_nat = at(63, 2 * P)
        gates = at(57, NB, PH * TOPK)
        w_q = at(64, PH, KD, 2 * P)
        ring = at(128, RING, 2 * D)
        idx_f = at(192, TOPK)
        top_v = at(192.25, 2, TOPK)
        soft = at(193, TOPK)

        def small(name, shape, dt=F32):
            return ctx.enter_context(nc.sbuf_tensor(name, [P] + shape, dt))

        cols = small("cols", [N_COLS])
        q_bias8 = small("q_bias8", [CC])
        ident = at(194, P)
        gates_flat = gates.rearrange("p a b -> p (a b)")
        zeros = small("zeros", [HALF], BF16)
        stats = small("stats", [2, 6])
        mv = small("mv", [2])
        std = small("std", [1])
        eps_col = small("eps_col", [1])
        rstd = small("rstd", [1])
        hcol = small("hcol", [TOPK])
        gcol = small("gcol", [TOPK])
        wcol = small("wcol", [TOPK])
        diag = at(195, DIAGS, P)
        idx_now = small("idx_now", [TOPK], U32)
        top_i = small("top_i", [2, TOPK], U32)
        pos = small("pos", [TOPK], U32)
        pos_ab = small("pos_ab", [TOPK, 2], U32)
        iota16 = small("iota16", [TOPK])
        iota_i = small("iota_i", [TOPK], mybir.dt.int32)
        top_s = small("top_s", [TOPK])
        den = small("den", [1])
        rden = small("rden", [1])

        ps = ctx.enter_context(nc.psum_tensor("ps", [P, 8, HALF], F32))
        ps_flat = ps[:, :, :].rearrange("p a b -> p (a b)")

        xT_in = [sem(f"xT_in{k}") for k in range(KD)]
        cols_in = sem("cols_in")
        w_in = [sem(f"w_in{j}") for j in range(4)]
        wv_in = sem("wv_in")
        bv_in = sem("bv_in")
        proj_done = sem("proj_done")
        psum_read = [sem(f"psum_read{j}") for j in range(4)]
        v_done = sem("v_done")
        qb_ready = sem("qb_ready")
        conv_step = sem("conv_step")
        conv_done = sem("conv_done")
        pad_ready = sem("pad_ready")
        consts = sem("consts")
        pool_step = sem("pool_step")
        mean_done = sem("mean_done")
        centred = sem("centred")
        squared = sem("squared")
        k_staged = sem("k_staged")
        v_staged = sem("v_staged")
        blk_staged = sem("blk_staged")
        q_zeroed = sem("q_zeroed")
        x1_staged = sem("x1_staged")
        qT_psum = sem("qT_psum")
        qT_ready = sem("qT_ready")
        var_done = sem("var_done")
        std_done = sem("std_done")
        rstd_done = sem("rstd_done")
        normed = sem("normed")
        swish_done = sem("swish_done")
        z_done = sem("z_done")
        abs_done = sem("abs_done")
        e_done = sem("e_done")
        l_done = sem("l_done")
        sp_done = sem("sp_done")
        sp_masked = sem("sp_masked")
        acc_done = sem("acc_done")
        suffix_done = sem("suffix_done")
        att_done = sem("att_done")
        att_masked = sem("att_masked")
        av_done = sem("av_done")
        out_read = sem("out_read")
        wmix_in = [sem(f"wmix_in{j}") for j in range(2)]
        gates_done = sem("gates_done")
        x_rounded = sem("x_rounded")
        x_split = sem("x_split")
        w1_rounded = sem("w1_rounded")
        w1_split = sem("w1_split")
        wv_rounded = sem("wv_rounded")
        wv_split = sem("wv_split")
        w_rounded = sem("w_rounded")
        w_split = sem("w_split")
        branch_done = sem("branch_done")
        sigs_ready = sem("sigs_ready")
        mix_step = sem("mix_step")
        mixed = [sem(f"mixed{j}") for j in range(2)]
        wout_in = [sem(f"wout_in{j}") for j in range(2)]
        rows_in = sem("rows_in")
        x_loaded = sem("x_loaded")
        wout_done = sem("wout_done")
        pre_read = sem("pre_read")
        ln1_step = sem("ln1_step")
        var1_ready = sem("var1_ready")
        std1_ready = sem("std1_ready")
        x1_ready = sem("x1_ready")
        wq_in = sem("wq_in")
        wq0_in = sem("wq0_in")
        wq_rest_in = sem("wq_rest_in")
        keys_in = sem("keys_in")
        rows2_in = sem("rows2_in")
        x1T_psum = sem("x1T_psum")
        x1T_ready = sem("x1T_ready")
        q_psum = sem("q_psum")
        q_ready = sem("q_ready")
        score_psum = sem("score_psum")
        score_ready = sem("score_ready")
        topk_step = sem("topk_step")
        idx_ready = sem("idx_ready")
        soft_step = sem("soft_step")
        shifted = sem("shifted")
        exp_ready = sem("exp_ready")
        gates_ready = sem("gates_ready")
        gathered = [sem(f"gathered{r}") for r in range(RING)]
        dots_done = sem("dots_done")
        gelu_step = sem("gelu_step")
        diag_ready = sem("diag_ready")
        expert_used = [sem(f"expert_used{r}") for r in range(RING)]
        y_read = sem("y_read")
        ln2_step = sem("ln2_step")
        var2_ready = sem("var2_ready")
        std2_ready = sem("std2_ready")
        out_ready = sem("out_ready")
        eps_ready = sem("eps_ready")
        iota_ready = sem("iota_ready")
        idx_copied = sem("idx_copied")
        stored = sem("stored")

        block = ctx.enter_context(nc.Block())

        TOPK_STEPS = 19

        @block.sync
        def _(sp_eng):
            sp_eng.dma_start(w_ring[:, 0, :, :].rearrange("p a b -> p (a b)"), w_proj_d[0, :, :]).then_inc(w_in[0], 16)
            for k in range(KD):
                sp_eng.dma_start(xT[:, k, :], xT_d[:, k, :]).then_inc(xT_in[k], 16)
            sp_eng.dma_start(cols[:, :], cols_d).then_inc(cols_in, 16)
            for j in range(1, 4):
                sp_eng.dma_start(w_ring[:, j, :, :].rearrange("p a b -> p (a b)"), w_proj_d[j, :, :]).then_inc(w_in[j], 16)
            sp_eng.dma_start(w_v, w_v_d).then_inc(wv_in, 16)
            sp_eng.dma_start(bv_row[0:1, :], bv_d).then_inc(bv_in, 16)
            sp_eng.dma_start(keysT.rearrange("p a b c -> p (a b c)"), keys_d).then_inc(keys_in, 16)
            with sp_eng.Fori(1, 4) as it:
                for j in range(4):
                    sp_eng.wait_ge(proj_done, (it - 1) * 4 + j + 1)
                    sp_eng.dma_start(w_ring[:, j, :, :].rearrange("p a b -> p (a b)"),
                                     w_proj_d[it * 4 + j, :, :]).then_inc(w_in[j], 16)
            sp_eng.wait_ge(v_done, NB)
            sp_eng.dma_start(w_mix[:, 1, :], w_mix_d[0, :, :]).then_inc(wmix_in[0], 16)
            sp_eng.wait_ge(out_read, START + PAIRS * 2)
            sp_eng.dma_start(w_mix[:, 0, :], w_mix_d[1, :, :]).then_inc(wmix_in[1], 16)
            with sp_eng.Fori(1, 4) as it:
                for j in range(2):
                    sp_eng.wait_ge(branch_done, it * 4 + 2 * j - 2)
                    sp_eng.dma_start(w_mix[:, 1 - j, :], w_mix_d[it * 2 + j, :, :]).then_inc(wmix_in[j], 16)
            sp_eng.wait_ge(branch_done, 2 * KD)
            sp_eng.dma_start(w_out[:, 0:CC, :], w_out_d[:, 0:CC, :]).then_inc(wout_in[0], 16)
            sp_eng.dma_start(w_out[:, CC:KD, :], w_out_d[:, CC:KD, :]).then_inc(wout_in[1], 16)
            sp_eng.dma_start(x_in, x_d[0:P, :]).then_inc(x_loaded, 16)
            sp_eng.dma_start(b_out_bc, b_out_d.partition_broadcast(P)).then_inc(rows_in, 16)
            sp_eng.dma_start(ln1_g_bc, ln1_g_d.partition_broadcast(P)).then_inc(rows_in, 16)
            sp_eng.dma_start(ln1_b_bc, ln1_b_d.partition_broadcast(P)).then_inc(rows_in, 16)
            sp_eng.dma_start(w_q[:, PH - 1, :, :], w_q_d[:, 0, :, :]).then_inc(wq_in, 16)
            sp_eng.dma_start(w_q[:, PH - 2, :, :], w_q_d[:, PH - 2, :, :]).then_inc(wq_rest_in, 16)
            with sp_eng.Fori(0, PH - 1) as h:
                sp_eng.wait_ge(q_psum, h + 1)
                sp_eng.dma_start(w_q[:, PH - 1, :, :], w_q_d[:, h + 1, :, :]).then_inc(wq_in, 16)
                sp_eng.wait_ge(x1_ready, START + h + 1)
                sp_eng.dma_start(x_in, x_d[bass.ds((h + 1) * P, P), :]).then_inc(x_loaded, 16)
            sp_eng.wait_ge(wout_done, START + NB)
            sp_eng.dma_start(w_q[:, 0, :, :], w_q_d[:, 0, :, :]).then_inc(wq0_in, 16)
            for h in range(1, 4):
                sp_eng.dma_start(w_q[:, h, :, :], w_q_d[:, h, :, :]).then_inc(wq_rest_in, 16)
            sp_eng.wait_ge(x1_ready, START + NB)
            for h in range(4, 6):
                sp_eng.dma_start(w_q[:, h, :, :], w_q_d[:, h, :, :]).then_inc(wq_rest_in, 16)
            sp_eng.dma_start(ln2_g_bc, ln2_g_d.partition_broadcast(P)).then_inc(rows2_in, 16)
            sp_eng.dma_start(ln2_b_bc, ln2_b_d.partition_broadcast(P)).then_inc(rows2_in, 16)
            with sp_eng.Fori(0, NB) as b:
                sp_eng.wait_ge(out_ready, b + 1)
                sp_eng.dma_start(out_d[bass.ds(b * P, P), :], pre2).then_inc(stored, 16)
            sp_eng.wait_ge(stored, 16 * START + 16 * NB)

        @block.gpsimd
        def _(pool):
            for s in (psum_read + expert_used + mixed +
                      [pre_read, wout_done, conv_done, att_done, sp_done, suffix_done, av_done, acc_done, out_read, z_done, x1_ready, q_ready,
                       qT_ready, score_ready, y_read, idx_ready, idx_copied, x1T_psum]):
                pool.sem_inc(s, START)
            pool.sem_inc(stored, 16 * START)
            pool.memset(conv_in[:, 0:PAD], 0.0).then_inc(pad_ready, 1)
            pool.memset(mean_w, 1.0 / CONV).then_inc(consts, 1)
            pool.memset(one_row[0:1, :], 1.0).then_inc(consts, 1)
            pool.memset(neg_ones, -1.0).then_inc(consts, 1)
            pool.memset(zeros[:, :], 0.0).then_inc(consts, 1)
            pool.memset(tri, -1.0).then_inc(pool_step, 1)
            pool.iota(iota_i[:, :], pattern=[[1, TOPK]], base=0, channel_multiplier=0).then_inc(consts, 1)
            pool.wait_ge(pool_step, 1)
            pool.affine_select(out=tri, in_=tri, compare_op=ALU.is_ge, fill=0.0, base=0,
                               pattern=[[-1, P]], channel_multiplier=1).then_inc(consts, 1)

            for j in range(4):
                pool.wait_ge(w1_rounded, j + 1)
                nc.gpsimd.tensor_tensor(w1_lo_r[:, j, :, :], w_ring[:, j, :, :], w1_hi_r[:, j, :, :].bitcast(F32),
                                        ALU.subtract).then_inc(w1_split, 1)
            with pool.Fori(1, CC) as it:
                for j in range(4):
                    wait_alone(pool, w1_rounded, it * 4 + j + 1, consts)
                    nc.gpsimd.tensor_tensor(w1_lo_r[:, j, :, :], w_ring[:, j, :, :], w1_hi_r[:, j, :, :].bitcast(F32),
                                            ALU.subtract).then_inc(w1_split, 1)
            for k in range(KD):
                pool.wait_ge(wv_rounded, k + 1)
                nc.gpsimd.tensor_tensor(wv_lo_r[:, k, :], w_v[:, k, :], wv_hi_r[:, k, :].bitcast(F32),
                                        ALU.subtract).then_inc(wv_split, 1)

            pool.wait_ge(var_done, 1)
            pool.wait_ge(psum_read[3], START + 6)
            pool.memset(q_pair[DH:P, 0, :], 0.0).then_inc(q_zeroed, 1)
            pool.memset(q_pair[0:DH, 1, :], 0.0).then_inc(q_zeroed, 1)
            with pool.Fori(0, PAIRS) as p:
                order = sorted([(u, 0) for u in DIAG_NO] + [(u + 1.5, 1) for u in DIAG_NO])
                for key, what in order:
                    u = int(key) if what == 0 else int(key - 1.5)
                    Q, kb, hd = UNITS[u]
                    c0 = kb * P - Q * HALF
                    if what == 0:
                        wait_alone(pool, sp_done, START + p * NU + u + 1, consts)
                        tile, signal = sp[:, u % 3, c0:c0 + P], sp_masked
                    else:
                        wait_alone(pool, att_done, START + p * NU + u + 1, consts)
                        tile, signal = att[:, u % 3, c0:c0 + P], att_masked
                    pool.affine_select(out=tile, in_=tile, compare_op=ALU.is_gt, fill=0.0, base=0,
                                       pattern=[[1, P]], channel_multiplier=-1).then_inc(signal, 1)

            pool.memset(ident, 0.0).then_inc(pool_step, 1)
            pool.wait_ge(pool_step, 2)
            pool.affine_select(out=ident, in_=ident, compare_op=ALU.not_equal, fill=1.0, base=0,
                               pattern=[[-1, P]], channel_multiplier=1).then_inc(consts, 1)

            with pool.Fori(0, NB * PH) as t:
                wait_alone(pool, idx_ready, START + t + 1, consts)
                for s in range(TOPK):
                    if s % RING == 0:
                        pool.tensor_copy(idx_now[:, s:s + RING],
                                         idx_f[:, s:s + RING]).then_inc(idx_copied, 1)
                        wait_alone(pool, idx_copied, START + t * 2 + (s // RING + 1), consts)
                    wait_alone(pool, expert_used[s % RING], START + t * 2 + s // RING, consts)
                    pool.indirect_dma_start(
                        out=ring[:, s % RING, :], out_offset=None, in_=uv_d,
                        in_offset=bass.IndirectOffsetOnAxis(ap=idx_now[:, s:s + 1], axis=0),
                    ).then_inc(gathered[s % RING], 16)

        @block.tensor
        def _(pe):
            pe.wait_ge(consts, 6)

            with pe.Fori(0, 4) as it:
                for j in range(4):
                    pe.wait_ge(w1_split, it * 4 + j + 1)
                    pe.wait_ge(psum_read[j], START + it)
                    for k in range(KD):
                        if j == 0:
                            pe.wait_ge(x_split, k + 1)
                        for h in range(2):
                            cs = slice(h * HALF, (h + 1) * HALF)
                            last = split_products(ps[:, 2 * j + h, :], (w1_hi_r[:, j, k, :], w1_lo_r[:, j, k, :]),
                                                  (x_hi_r[:, k, cs], x_lo_r[:, k, cs]), k == 0, k == KD - 1)
                    last.then_inc(proj_done, 1)
            pe.wait_ge(wv_in, 16)
            pe.wait_ge(bv_in, 16)
            def value_block(b):
                j = b % 4
                if b >= 4:
                    pe.wait_ge(psum_read[j], START + 5)
                nc.tensor.matmul(ps[:, j, :], one_row[0:1, :], bv_row[0:1, :], start=True, stop=False)
                for k in range(KD):
                    if b == 0:
                        pe.wait_ge(wv_split, k + 1)
                    ts = slice(b * P, (b + 1) * P)
                    last = split_products(ps[:, j, :], (x_hi_r[:, k, ts], x_lo_r[:, k, ts]),
                                          (wv_hi_r[:, k, :], wv_lo_r[:, k, :]), False, k == KD - 1)
                last.then_inc(v_done, 1)

            for j in range(4):
                pe.wait_ge(psum_read[j], START + CC)
            for b in range(6):
                value_block(b)
            pe.wait_ge(conv_done, START + CC)
            for h in range(2):
                for c in range(CC):
                    last = nc.tensor.matmul(ps[:, 4 + h, :], mean_w, conv[:, c, h * HALF:(h + 1) * HALF],
                                            start=(c == 0), stop=(c == CC - 1))
            last.then_inc(mean_done, 1)
            value_block(6)
            for c in range(CC):
                pe.wait_ge(squared, c + 1)
                for h in range(2):
                    last = nc.tensor.matmul(ps[:, 6 + h, :], mean_w, conv_sq[:, c, h * HALF:(h + 1) * HALF],
                                            start=(c == 0), stop=(c == CC - 1))
            last.then_inc(var_done, 1)
            value_block(7)

            pe.wait_ge(centred, CC)
            pe.wait_ge(std_done, 1)
            for j in range(4):
                pe.wait_ge(psum_read[j], START + 6)

            def score_mm(p, u):
                Q, kb, hd = UNITS[u]
                c0 = max(0, kb * P - Q * HALF)
                pe.wait_ge(att_done, START + p * NU + (u - Z_BANKS + 1 if u >= Z_BANKS else 0))
                nc.tensor.matmul(ps[:, z_bank(u), c0:HALF], k_pair[:, kb * P:(kb + 1) * P],
                                 q_pair[:, hd, Q * HALF + c0:(Q + 1) * HALF],
                                 start=True, stop=True, skip_group_check=True).then_inc(z_done, 1)

            def suffix_mm(p, u):
                Q, kb, hd = UNITS[u]
                c0 = max(0, kb * P - Q * HALF)
                diagonal = kb >= 4 * Q
                old = c0 + P if diagonal else 0
                if diagonal:
                    pe.wait_ge(sp_masked, p * N_DIAG + DIAG_NO[u] + 1)
                else:
                    pe.wait_ge(sp_done, START + p * NU + u + 1)
                first = kb == 4 * Q + 3
                last = nc.tensor.matmul(ps[:, z_bank(u), c0:HALF], tri, sp[:, u % 3, c0:HALF],
                                        start=False, stop=True, skip_group_check=True)
                if not first:
                    pe.wait_ge(acc_done, START + p * N_ACC + ACC_NO[u - 2] + 1)
                    last = nc.tensor.matmul(ps[:, z_bank(u), old:HALF], neg_ones, acc[:, hd, (kb + 1) % 2, old:HALF],
                                            start=False, stop=True, skip_group_check=True)
                last.then_inc(suffix_done, 1)

            def value_mm(p, u):
                Q, kb, hd = UNITS[u]
                c0 = max(0, kb * P - Q * HALF)
                first = kb == 4 * Q + 3
                if kb >= 4 * Q:
                    pe.wait_ge(att_masked, p * N_DIAG + DIAG_NO[u] + 1)
                else:
                    pe.wait_ge(att_done, START + p * NU + u + 1)
                if first and hd == 0:
                    pe.wait_ge(out_read, START + p * 2)
                r = slice(hd * DH, (hd + 1) * DH)
                nc.tensor.matmul(ps[r, 4 + Q, c0:HALF], v_pair[:, kb, hd * DH:(hd + 1) * DH],
                                 att[:, u % 3, c0:HALF],
                                 start=first, stop=(kb == 0), skip_group_check=True).then_inc(av_done, 1)

            with pe.Fori(0, PAIRS) as p:
                pe.wait_ge(k_staged, p + 1)
                for u in range(Z_AHEAD):
                    score_mm(p, u)
                pe.wait_ge(v_staged, p + 1)
                for t in range(NU + VALUE_LAG):
                    if t + Z_AHEAD < NU:
                        score_mm(p, t + Z_AHEAD)
                    if t < NU:
                        suffix_mm(p, t)
                    if t >= VALUE_LAG:
                        value_mm(p, t - VALUE_LAG)

            pe.wait_ge(swish_done, CC)
            pe.wait_ge(out_read, START + PAIRS * 2)
            with pe.Fori(0, KD // 2) as i:
                for j in range(2):
                    pe.wait_ge(wmix_in[j], (i + 1) * 16)
                    for h in range(2):
                        cs = slice(h * HALF, (h + 1) * HALF)
                        pe.wait_ge(mixed[h], START + i * 2 + j)
                        for g in range(2):
                            if h == 0:
                                pe.wait_ge(w_split, i * 4 + (j * 2 + g + 1))
                            for k in range(KD):
                                ws = slice(g * D + k * P, g * D + (k + 1) * P)
                                last = split_products(ps[:, 4 * h + g, :], (w_hi_r[:, j, ws], w_lo_r[:, 1 - j, ws]),
                                                      (x_hi_r[:, k, cs], x_lo_r[:, k, cs]), k == 0, k == KD - 1)
                        last.then_inc(gates_done, 1)
                        for y, src in ((0, conv), (1, attT)):
                            for k in range(CC):
                                o = 2 * D + y * HALF + k * P
                                last = nc.tensor.matmul(ps[:, 4 * h + 2 + y, :], w_mix[:, 1 - j, o:o + P],
                                                        src[:, k, cs], start=(k == 0), stop=(k == CC - 1))
                        last.then_inc(branch_done, 1)

            def wout_mm(b, k0, k1):
                if k0 == 0:
                    wait_alone(pe, blk_staged, b + 1, consts)
                    pe.wait_ge(pre_read, START + b)
                for k in range(k0, k1):
                    for h in range(2):
                        last = nc.tensor.matmul(ps[:, 6 + h, :], mix_blk[:, k, :],
                                                w_out[:, k, h * HALF:(h + 1) * HALF],
                                                start=(k == 0), stop=(k == KD - 1))
                if k1 == KD:
                    last.then_inc(wout_done, 1)

            def transposes(b):
                pe.wait_ge(x1_staged, b + 1)
                for k in range(KD):
                    last = nc.tensor.transpose(ps_flat[:, k * P:(k + 1) * P], x1_blk[:, k * P:(k + 1) * P], ident)
                last.then_inc(x1T_psum, 1)

            def queries(r, place):
                pe.wait_ge(q_ready, START + r)
                for k in range(KD):
                    last = nc.tensor.matmul(ps[:, 2, 0:2 * P], x1T[:, k, :], w_q[:, place, k, :],
                                            start=(k == 0), stop=(k == KD - 1))
                last.then_inc(q_psum, 1)

            def query_transposes(r):
                pe.wait_ge(q_ready, START + r + 1)
                pe.wait_ge(qT_ready, START + r)
                for half in range(2):
                    last = nc.tensor.transpose(ps[:, 2, (2 + half) * P:(3 + half) * P],
                                               q_nat[:, half * P:(half + 1) * P], ident)
                last.then_inc(qT_psum, 1)

            def scores(r, h):
                pe.wait_ge(qT_ready, START + r + 1)
                pe.wait_ge(score_ready, START + r)
                for half in range(2):
                    last = nc.tensor.matmul(ps[:, 3, half * P:(half + 1) * P], q_sb[:, half, :],
                                            keysT[:, h, half, :], start=True, stop=True)
                last.then_inc(score_psum, 1)

            def experts(t, g):
                for s in range(2 * g, 2 * g + 2):
                    pe.wait_ge(diag_ready, t * TOPK + s + 1)
                    for h in range(2):
                        last = nc.tensor.matmul(ps[:, 4 + h, :], diag[:, s % DIAGS, :],
                                                ring[:, s % RING, D + h * HALF:D + (h + 1) * HALF],
                                                start=False, stop=False, skip_group_check=True)
                    last.then_inc(expert_used[s % RING], 1)

            def clear_y(b):
                pe.wait_ge(y_read, START + b)
                for h in range(2):
                    nc.tensor.matmul(ps[:, 4 + h, :], zeros[:, 0:P], zeros[:, :], start=True, stop=True,
                                     skip_group_check=True)

            def experts_and_retrieval(t, r, h, place, b5=None):
                for g in range(TOPK // 2):
                    if r is not None and g == 0:
                        queries(r, place)
                    if r is not None and g == 1:
                        query_transposes(r)
                    if r is not None and g == 2:
                        scores(r, h)
                    if b5 is not None and 1 <= g <= 4:
                        wout_mm(b5, 2 * g - 2, 2 * g)
                    experts(t, g)

            for h in range(2):
                pe.wait_ge(mixed[h], START + KD)
            pe.wait_ge(wout_in[0], 16)
            wout_mm(0, 0, CC)
            pe.wait_ge(wout_in[1], 16)
            wout_mm(0, CC, KD)
            pe.wait_ge(consts, 7)
            pe.wait_ge(keys_in, 16)
            pe.wait_ge(wq_in, 16)
            transposes(0)
            pe.wait_ge(x1T_ready, 1)
            queries(0, PH - 1)
            query_transposes(0)
            scores(0, 0)
            clear_y(0)
            with pe.Fori(0, PH - 1) as h:
                wait_alone(pe, wq_in, 16 * h + 32, consts)
                experts_and_retrieval(h, h + 1, h + 1, PH - 1, h + 1)
            transposes(1)
            pe.wait_ge(x1T_ready, 2)
            pe.wait_ge(wq0_in, 16)
            experts_and_retrieval(PH - 1, PH, 0, 0)
            pe.wait_ge(wq_rest_in, 16 * (PH - 2))
            with pe.Fori(1, NB - 1) as b:
                clear_y(b)
                with pe.Fori(0, PH - 1) as h:
                    experts_and_retrieval(b * PH + h, b * PH + h + 1, h + 1, h + 1)
                transposes(b + 1)
                wait_alone(pe, x1T_ready, b + 2, consts)
                experts_and_retrieval(b * PH + (PH - 1), b * PH + PH, 0, 0)
            clear_y(NB - 1)
            with pe.Fori(0, PH - 1) as h:
                experts_and_retrieval(h + (NB - 1) * PH, h + ((NB - 1) * PH + 1), h + 1, h + 1)
            experts_and_retrieval(NB * PH - 1, None, None, None)

        @block.scalar
        def _(act):
            def round_w1(j):
                nc.scalar.activation(w1_hi_r[:, j, :, :], w_ring[:, j, :, :], ACT.Copy).then_inc(w1_rounded, 1)

            act.wait_ge(w_in[0], 16)
            round_w1(0)
            for k in range(KD):
                act.wait_ge(xT_in[k], 16)
                nc.scalar.activation(x_hi_r[:, k, :], xT[:, k, :], ACT.Copy).then_inc(x_rounded, 1)
            for j in range(1, 4):
                act.wait_ge(w_in[j], 16)
                round_w1(j)
            act.wait_ge(cols_in, 16)
            act.wait_ge(eps_ready, 1)
            nc.scalar.mul(q_bias8[:, :], cols[:, C_Q:C_Q + CC], DH ** -0.5).then_inc(qb_ready, 1)
            act.wait_ge(wv_in, 16)
            for k in range(KD):
                nc.scalar.activation(wv_hi_r[:, k, :], w_v[:, k, :], ACT.Copy).then_inc(wv_rounded, 1)

            act.wait_ge(qb_ready, 1)

            def projected(c, next_weights):
                def next_w1(j):
                    if next_weights:
                        wait_alone(act, w_in[j], c * 16 + 32, cols_in)
                        round_w1(j)

                act.wait_ge(psum_read[0], START + c)
                wait_alone(act, proj_done, c * 4 + 2, cols_in)
                nc.scalar.activation(glu_gate, ps_flat[:, 2 * HALF:4 * HALF], ACT.Sigmoid,
                                     bias=cols[:, bass.ds(c + C_G, 1)]).then_inc(psum_read[1], 1)
                next_w1(0)
                wait_alone(act, proj_done, c * 4 + 3, cols_in)
                nc.scalar.activation(qT[:, c, :], ps_flat[:, 4 * HALF:6 * HALF], ACT.Identity,
                                     bias=q_bias8[:, bass.ds(c, 1)], scale=DH ** -0.5).then_inc(psum_read[2], 1)
                next_w1(1)
                wait_alone(act, proj_done, c * 4 + 4, cols_in)
                nc.scalar.activation(kT[:, c, :], ps_flat[:, 6 * HALF:8 * HALF], ACT.Identity,
                                     bias=cols[:, bass.ds(c + C_K, 1)]).then_inc(psum_read[3], 1)
                next_w1(2)
                next_w1(3)

            with act.Fori(0, CC - 1) as c:
                projected(c, True)
            projected(CC - 1, False)

            def value_out(b):
                act.wait_ge(v_done, b + 1)
                nc.scalar.activation(v_sb[:, b, :], ps[:, b % 4, :], ACT.Copy).then_inc(psum_read[b % 4], 1)

            for b in range(4):
                value_out(b)
            for c in range(CC):
                act.wait_ge(centred, c + 1)
                nc.scalar.activation(conv_sq[:, c, :], conv[:, c, :], ACT.Square).then_inc(squared, 1)
            act.wait_ge(var_done, 1)
            nc.scalar.activation(rstd_row, ps_flat[:, 6 * HALF:8 * HALF], ACT.Sqrt,
                                 bias=eps_col[:, :]).then_inc(std_done, 1)
            for c in range(CC):
                act.wait_ge(normed, c + 1)
                nc.scalar.activation(conv[:, c, :], conv[:, c, :], ACT.Silu, bias=cols[:, C_LB + c:C_LB + c + 1],
                                     scale=cols[:, C_LG + c:C_LG + c + 1]).then_inc(swish_done, 1)
            for b in range(4, NB):
                value_out(b)

            def soft_log(p, u):
                Q, kb, hd = UNITS[u]
                c0 = max(0, kb * P - Q * HALF)
                act.wait_ge(z_done, START + p * NU + u + 1)
                act.wait_ge(sp_done, START + p * NU + (u - 3 if u >= 4 else 0))
                nc.scalar.activation(el[:, u % 4, c0:HALF], ps[:, z_bank(u), c0:HALF], ACT.Abs).then_inc(abs_done, 1)
                act.wait_ge(abs_done, p * NU + u + 1)
                nc.scalar.activation(el[:, u % 4, c0:HALF], el[:, u % 4, c0:HALF], ACT.Exp, scale=-1.0).then_inc(e_done, 1)
                act.wait_ge(e_done, p * NU + u + 1)
                nc.scalar.activation(el[:, u % 4, c0:HALF], el[:, u % 4, c0:HALF], ACT.Ln, bias=1.0).then_inc(l_done, 1)

            def weights(p, u):
                Q, kb, hd = UNITS[u]
                c0 = max(0, kb * P - Q * HALF)
                act.wait_ge(suffix_done, START + p * NU + u + 1)
                act.wait_ge(av_done, START + p * NU + (u - 2 if u >= 3 else 0))
                nc.scalar.activation(att[:, u % 3, c0:HALF], ps[:, z_bank(u), c0:HALF], ACT.Exp).then_inc(att_done, 1)

            def evacuate(p, Q, last_unit):
                act.wait_ge(av_done, START + p * NU + last_unit + 1)
                nc.scalar.activation(attT[:, p, Q * HALF:(Q + 1) * HALF], ps[:, 4 + Q, :], ACT.Copy).then_inc(out_read, 1)

            act.preload_act_table_set("natural_log_exp_and_others")
            with act.Fori(0, PAIRS) as p:
                soft_log(p, 0)
                soft_log(p, 1)
                for t in range(NU):
                    if t + 2 < NU:
                        soft_log(p, t + 2)
                    weights(p, t)
                    if t == 10:
                        evacuate(p, 0, 7)
                evacuate(p, 1, NU - 1)

            def round_w(j, g):
                nc.scalar.activation(w_hi_r[:, j, g * D:(g + 1) * D], w_mix[:, 1 - j, g * D:(g + 1) * D],
                                     ACT.Copy).then_inc(w_rounded, 1)

            def sigmoids(m):
                for h in range(2):
                    act.wait_ge(mixed[h], START + m)
                    wait_alone(act, gates_done, m * 2 + h + 1, cols_in)
                    for g in range(2):
                        nc.scalar.activation(gate_tmp[:, h, g, :], ps[:, 4 * h + g, :], ACT.Sigmoid,
                                             bias=cols[:, bass.ds(m + (C_GA + g * KD), 1)]).then_inc(sigs_ready, 1)

            act.wait_ge(wmix_in[0], 16)
            round_w(0, 0)
            round_w(0, 1)
            act.wait_ge(wmix_in[1], 16)
            round_w(1, 0)
            round_w(1, 1)
            with act.Fori(0, KD // 2 - 1) as i:
                for j in range(2):
                    sigmoids(i * 2 + j)
                    wait_alone(act, wmix_in[j], i * 16 + 32, cols_in)
                    for g in range(2):
                        round_w(j, g)
            for m in range(KD - 2, KD):
                sigmoids(m)
            def stage_mix(b):
                wait_alone(act, wout_done, START + b, cols_in)
                nc.scalar.activation(mix_blk.rearrange("p a b -> p (a b)"), x1[:, b, :],
                                     ACT.Copy).then_inc(blk_staged, 1)

            def std1(b):
                act.wait_ge(var1_ready, b + 1)
                nc.scalar.activation(std[:, :], mv[:, 1:2], ACT.Sqrt, bias=eps_col[:, :]).then_inc(std1_ready, 1)

            def x1_stage(b):
                act.wait_ge(x1T_psum, START + b)
                nc.scalar.activation(x1_blk, x1[:, b, :], ACT.Copy).then_inc(x1_staged, 1)

            def x1T_out(b):
                act.wait_ge(x1T_psum, START + b + 1)
                nc.scalar.activation(x1T.rearrange("p a b -> p (a b)"), ps_flat[:, 0:D], ACT.Copy).then_inc(x1T_ready, 1)

            def q_out(r):
                act.wait_ge(q_psum, r + 1)
                nc.scalar.activation(q_nat, ps[:, 2, 0:2 * P], ACT.Copy).then_inc(q_ready, 1)

            def qT_out(r):
                act.wait_ge(qT_psum, r + 1)
                nc.scalar.activation(q_sb.rearrange("p a b -> p (a b)"), ps[:, 2, 2 * P:4 * P], ACT.Copy).then_inc(qT_ready, 1)

            def score_out(r):
                act.wait_ge(score_psum, r + 1)
                act.wait_ge(idx_ready, START + r)
                nc.scalar.activation(score.rearrange("p a b -> p (a b)"), ps[:, 3, 0:2 * NKEY],
                                     ACT.Copy).then_inc(score_ready, 1)

            def soft_exp(r):
                act.wait_ge(shifted, r + 1)
                nc.scalar.activation(soft, soft, ACT.Exp, accum_out=den[:, :]).then_inc(exp_ready, 1)

            def expert_weights(t, g, steps):
                act.wait_ge(dots_done, t * (TOPK // 2) + g + 1)
                s0 = 2 * g
                steps.link(nc.scalar.activation(gcol[:, s0:s0 + 2], hcol[:, s0:s0 + 2], ACT.Gelu))
                for s in (s0, s0 + 1):
                    last = nc.scalar.activation(wcol[:, s:s + 1], gcol[:, s:s + 1], ACT.Copy,
                                                scale=gates_flat[:, bass.ds(t * TOPK + s, 1)])
                steps.link(last)
                for s in (s0, s0 + 1):
                    f = s - DIAGS
                    act.wait_ge(expert_used[f % RING], START + t * 2 + (f // RING + 1 if f >= 0 else 0))
                    nc.scalar.activation(diag[:, s % DIAGS, :], ident, ACT.Copy,
                                         scale=wcol[:, s:s + 1]).then_inc(diag_ready, 1)

            def finish_std(b):
                act.wait_ge(var2_ready, b + 1)
                nc.scalar.activation(std[:, :], mv[:, 1:2], ACT.Sqrt, bias=eps_col[:, :]).then_inc(std2_ready, 1)

            def experts_and_retrieval(t, r, b5=None):
                steps = Steps(act, gelu_step, t * TOPK)
                if b5 is not None:
                    stage_mix(b5)
                for g in range(TOPK // 2):
                    if r is not None and g == 7:
                        soft_exp(r)
                    expert_weights(t, g, steps)
                    if r is not None and g == 0:
                        q_out(r)
                    if r is not None and g == 1:
                        qT_out(r)
                        score_out(r)
                assert steps.n == TOPK
                if b5 is not None:
                    std1(b5)

            act.wait_ge(consts, 7)
            for h in range(2):
                act.wait_ge(mixed[h], START + KD)
            stage_mix(0)
            std1(0)
            act.wait_ge(x1_ready, START + 1)
            x1_stage(0)
            x1T_out(0)
            q_out(0)
            qT_out(0)
            score_out(0)
            soft_exp(0)
            with act.Fori(0, PH - 1) as h:
                act.wait_ge(gates_ready, h + 1)
                experts_and_retrieval(h, h + 1, h + 1)
            act.wait_ge(x1_ready, START + NB)
            x1_stage(1)
            x1T_out(1)
            act.wait_ge(gates_ready, PH)
            experts_and_retrieval(PH - 1, PH)
            finish_std(0)
            with act.Fori(1, NB - 1) as b:
                with act.Fori(0, PH - 1) as h:
                    act.wait_ge(gates_ready, b * PH + h + 1)
                    experts_and_retrieval(b * PH + h, b * PH + h + 1)
                x1_stage(b + 1)
                x1T_out(b + 1)
                act.wait_ge(gates_ready, b * PH + PH)
                experts_and_retrieval(b * PH + (PH - 1), b * PH + PH)
                finish_std(b)
            with act.Fori(0, PH - 1) as h:
                act.wait_ge(gates_ready, h + ((NB - 1) * PH + 1))
                experts_and_retrieval(h + (NB - 1) * PH, h + ((NB - 1) * PH + 1))
            act.wait_ge(gates_ready, NB * PH)
            experts_and_retrieval(NB * PH - 1, None)
            finish_std(NB - 1)

        @block.vector
        def _(dve):
            nc.vector.memset(eps_col[:, :], EPS).then_inc(eps_ready, 1)
            for k in range(KD):
                dve.wait_ge(x_rounded, k + 1)
                nc.vector.tensor_tensor(x_lo_r[:, k, :], xT[:, k, :], x_hi_r[:, k, :].bitcast(F32),
                                        ALU.subtract).then_inc(x_split, 1)
            dve.wait_ge(cols_in, 16)
            dve.wait_ge(pad_ready, 1)
            with dve.Fori(0, CC) as c:
                dve.wait_ge(proj_done, c * 4 + 1)
                dve.wait_ge(psum_read[1], START + c + 1)
                dve.wait_ge(conv_done, START + c)
                nc.vector.scalar_tensor_tensor(
                    out=conv_in[:, PAD:PAD + S], in0=ps_flat[:, 0:2 * HALF], scalar=cols[:, bass.ds(c + C_A, 1)],
                    in1=glu_gate, op0=ALU.add, op1=ALU.mult).then_inc(psum_read[0], 1)
                dve.wait_ge(psum_read[0], START + c + 1)
                steps = Steps(dve, conv_step, c * PAD)
                steps.link(nc.vector.tensor_scalar(conv[:, c, :], conv_in[:, 0:S],
                                                   cols[:, bass.ds(c * TAPS + C_CW, 1)],
                                                   cols[:, bass.ds(c + C_CB, 1)], ALU.mult, ALU.add))
                for k in range(1, TAPS):
                    ins = nc.vector.scalar_tensor_tensor(
                        out=conv[:, c, :], in0=conv_in[:, k:k + S], scalar=cols[:, bass.ds(c * TAPS + (C_CW + k), 1)],
                        in1=conv[:, c, :], op0=ALU.mult, op1=ALU.add)
                    if k < TAPS - 1:
                        steps.link(ins)
                ins.then_inc(conv_done, 1)
                assert steps.n == PAD
            dve.wait_ge(conv_done, START + CC)
            dve.wait_ge(mean_done, 1)
            for c in range(CC):
                nc.vector.tensor_tensor(conv[:, c, :], conv[:, c, :], ps_flat[:, 4 * HALF:6 * HALF],
                                        ALU.subtract).then_inc(centred, 1)
            dve.wait_ge(std_done, 1)
            nc.vector.reciprocal(rstd_row, rstd_row).then_inc(rstd_done, 1)
            dve.wait_ge(rstd_done, 1)
            dve.wait_ge(centred, CC)
            for c in range(CC):
                nc.vector.tensor_tensor(conv[:, c, :], conv[:, c, :], rstd_row, ALU.mult).then_inc(normed, 1)
            dve.wait_ge(normed, CC)

            def softplus(p, u):
                Q, kb, hd = UNITS[u]
                c0 = max(0, kb * P - Q * HALF)
                dve.wait_ge(l_done, p * NU + u + 1)
                dve.wait_ge(suffix_done, START + p * NU + (u - 2 if u >= 3 else 0))
                dve.wait_ge(acc_done, START + p * N_ACC + (sum(v <= u - 3 for v in ACC_NO) if u >= 3 else 0))
                nc.vector.scalar_tensor_tensor(out=sp[:, u % 3, c0:HALF], in0=ps[:, z_bank(u), c0:HALF], scalar=0.0,
                                               in1=el[:, u % 4, c0:HALF], op0=ALU.max, op1=ALU.add).then_inc(sp_done, 1)

            def accumulate(p, u):
                Q, kb, hd = UNITS[u]
                if kb == 0:
                    return
                c0 = max(0, kb * P - Q * HALF)
                diagonal = kb >= 4 * Q
                old = c0 + P if diagonal else 0
                first = kb == 4 * Q + 3
                if diagonal:
                    dve.wait_ge(sp_masked, p * N_DIAG + DIAG_NO[u] + 1)
                    ins = nc.vector.tensor_copy(acc[:, hd, kb % 2, c0:old], sp[:, u % 3, c0:old])
                else:
                    dve.wait_ge(sp_done, START + p * NU + u + 1)
                if not first:
                    dve.wait_ge(acc_done, START + p * N_ACC + ACC_NO[u - 2] + 1)
                    ins = nc.vector.tensor_tensor(acc[:, hd, kb % 2, old:HALF], acc[:, hd, (kb + 1) % 2, old:HALF],
                                                  sp[:, u % 3, old:HALF], ALU.add)
                ins.then_inc(acc_done, 1)

            dve.wait_ge(psum_read[3], START + 6)
            dve.wait_ge(q_zeroed, 2)
            with dve.Fori(0, PAIRS) as p:
                dve.wait_ge(z_done, START + p * NU)
                nc.vector.tensor_copy(k_pair, kT[:, p, :])
                for hd in range(2):
                    r = slice(hd * DH, (hd + 1) * DH)
                    last = nc.vector.tensor_copy(q_pair[r, hd, :], qT[r, p, :])
                last.then_inc(k_staged, 1)
                dve.wait_ge(av_done, START + p * NU)
                nc.vector.tensor_copy(v_pair, v_sb[:, :, bass.ds(p * P, P)]).then_inc(v_staged, 1)
                softplus(p, 0)
                for t in range(NU):
                    if t + 1 < NU:
                        softplus(p, t + 1)
                    accumulate(p, t)

            def split_w(j, g, turn):
                gs = slice(g * D, (g + 1) * D)
                dve.wait_ge(w_rounded, turn * 2 + g + 1)
                nc.vector.tensor_tensor(w_lo_r[:, 1 - j, gs], w_mix[:, 1 - j, gs], w_hi_r[:, j, gs].bitcast(F32),
                                        ALU.subtract).then_inc(w_split, 1)

            def mix(m):
                for h in range(2):
                    dve.wait_ge(sigs_ready, m * 4 + 2 * h + 2)
                    dve.wait_ge(branch_done, m * 2 + h + 1)
                    nc.vector.scalar_tensor_tensor(out=gate_tmp[:, h, 0, :], in0=ps[:, 4 * h + 2, :],
                                                   scalar=cols[:, bass.ds(m + C_PW, 1)], in1=gate_tmp[:, h, 0, :],
                                                   op0=ALU.add, op1=ALU.mult)
                    nc.vector.tensor_tensor(gate_tmp[:, h, 1, :], ps[:, 4 * h + 3, :], gate_tmp[:, h, 1, :],
                                            ALU.mult).then_inc(mix_step, 1)
                    dve.wait_ge(mix_step, m * 2 + h + 1)
                    nc.vector.tensor_tensor(mixT[:, h * CC:(h + 1) * CC, m, :],
                                            gate_tmp[:, h, 0, :].rearrange("p (b t) -> p b t", t=P),
                                            gate_tmp[:, h, 1, :].rearrange("p (b t) -> p b t", t=P),
                                            ALU.add).then_inc(mixed[h], 1)

            split_w(0, 0, 0)
            split_w(0, 1, 0)
            split_w(1, 0, 1)
            split_w(1, 1, 1)
            with dve.Fori(0, KD // 2 - 1) as i:
                for j in range(2):
                    mix(i * 2 + j)
                    for g in range(2):
                        split_w(j, g, i * 2 + (j + 2))
            for m in range(KD - 2, KD):
                mix(m)

            def layer_norm(tile, steps, var_ready, std_ready, turn, g_bc, b_bc, out):
                for h in range(2):
                    last = nc.vector.bn_stats(stats[:, h, :], tile[:, h * HALF:(h + 1) * HALF])
                steps.link(last)
                nc.vector.bn_aggr(mv[:, :], stats[:, :, :].rearrange("p a b -> p (a b)")).then_inc(var_ready, 1)
                dve.wait_ge(std_ready, turn + 1)
                steps.link(nc.vector.reciprocal(rstd[:, :], std[:, :]))
                steps.link(nc.vector.tensor_scalar(tile, tile, mv[:, 0:1], rstd[:, 0:1], ALU.subtract, ALU.mult))
                steps.link(nc.vector.tensor_tensor(tile, tile, g_bc, ALU.mult))
                return nc.vector.tensor_tensor(out, tile, b_bc, ALU.add)

            def x1_block(b):
                steps = Steps(dve, ln1_step, b * 5, consts)
                dve.wait_ge(wout_done, START + b + 1)
                dve.wait_ge(x_loaded, (b + 1) * 16)
                nc.vector.scalar_tensor_tensor(out=x_in, in0=x_in, scalar=ALPHA, in1=ps_flat[:, 6 * HALF:8 * HALF],
                                               op0=ALU.mult, op1=ALU.add).then_inc(pre_read, 1)
                dve.wait_ge(pre_read, START + b + 1)
                steps.link(nc.vector.tensor_tensor(x_in, x_in, b_out_bc, ALU.add))
                layer_norm(x_in, steps, var1_ready, std1_ready, b, ln1_g_bc, ln1_b_bc,
                           x1[:, b, :]).then_inc(x1_ready, 1)
                assert steps.n == 5

            dve.wait_ge(consts, 6)
            nc.vector.tensor_copy(iota16[:, :], iota_i[:, :]).then_inc(iota_ready, 1)
            dve.wait_ge(iota_ready, 1)

            def topk_half(steps, half):
                s_half = score[:, half, :]
                steps.link(nc.vector.max(top_v[:, half, 0:8], s_half))
                steps.link(nc.vector.max_index(top_i[:, half, 0:8], top_v[:, half, 0:8], s_half))
                steps.link(nc.vector.match_replace(s_half, top_v[:, half, 0:8], s_half, NEG))
                steps.link(nc.vector.max(top_v[:, half, 8:16], s_half))
                steps.link(nc.vector.max_index(top_i[:, half, 8:16], top_v[:, half, 8:16], s_half))

            def topk_pairs(steps, r):
                steps.link(nc.vector.tensor_tensor(cand, top_v[:, 0, :].unsqueeze(2).to_broadcast([P, TOPK, TOPK]),
                                                   top_v[:, 1, :].unsqueeze(1).to_broadcast([P, TOPK, TOPK]), ALU.add))
                cf = cand.rearrange("p a b -> p (a b)")
                g0, g1 = top_s[:, 0:8], top_s[:, 8:16]
                steps.link(nc.vector.max(g0, cf))
                steps.link(nc.vector.max_index(pos[:, 0:8], g0, cf))
                steps.link(nc.vector.match_replace(cf, g0, cf, NEG))
                steps.link(nc.vector.max(g1, cf))
                steps.link(nc.vector.max_index(pos[:, 8:16], g1, cf))
                nc.vector.tensor_scalar(soft, top_s[:, :], top_s[:, 0:1], None, ALU.subtract).then_inc(shifted, 1)

            def expert_index(steps, r):
                nc.vector.tensor_scalar(top_i[:, 0, :], top_i[:, 0, :], 7, None, ALU.logical_shift_left)
                nc.vector.tensor_scalar(pos_ab[:, :, 0], pos[:, :], 4, None, ALU.logical_shift_right)
                steps.link(nc.vector.tensor_scalar(pos_ab[:, :, 1], pos[:, :], 15, None, ALU.bitwise_and))
                oh = onehot.rearrange("p k (a j) -> p k a j", a=2)
                steps.link(nc.vector.tensor_tensor(
                    oh, pos_ab[:, :, :].unsqueeze(3).to_broadcast([P, TOPK, 2, TOPK]),
                    iota16[:, :].unsqueeze(1).unsqueeze(1).to_broadcast([P, TOPK, 2, TOPK]), ALU.is_equal))
                steps.link(nc.vector.tensor_tensor(
                    oh, oh, top_i[:, :, :].unsqueeze(1).to_broadcast([P, TOPK, 2, TOPK]), ALU.mult))
                wait_alone(dve, idx_copied, START + r * 2, consts)
                nc.vector.tensor_reduce(idx_f, onehot, AX_X, ALU.add).then_inc(idx_ready, 1)

            def softmax(r):
                dve.wait_ge(exp_ready, r + 1)
                nc.vector.reciprocal(rden[:, :], den[:, :]).then_inc(soft_step, 1)
                dve.wait_ge(soft_step, r + 1)
                nc.vector.tensor_scalar(gates_flat[:, bass.ds(r * TOPK, TOPK)], soft, rden[:, 0:1], None,
                                        ALU.mult).then_inc(gates_ready, 1)

            def dots(b, t, g):
                for s in range(2 * g, 2 * g + 2):
                    dve.wait_ge(gathered[s % RING], (t * 2 + (s // RING + 1)) * 16)
                    last = nc.vector.scalar_tensor_tensor(
                        out=ring[:, s % RING, 0:D], in0=x1[:, b, :], scalar=1.0, in1=ring[:, s % RING, 0:D],
                        op0=ALU.mult, op1=ALU.mult, accum_out=hcol[:, s:s + 1])
                last.then_inc(dots_done, 1)

            def finish(b):
                steps = Steps(dve, ln2_step, b * 4, consts)
                dve.wait_ge(expert_used[RING - 1], START + b * 2 * PH + 2 * PH)
                dve.wait_ge(expert_used[RING - 2], START + b * 2 * PH + 2 * PH)
                dve.wait_ge(stored, 16 * START + b * 16)
                nc.vector.scalar_tensor_tensor(out=pre2, in0=x1[:, b, :], scalar=ALPHA,
                                               in1=ps_flat[:, 4 * HALF:6 * HALF],
                                               op0=ALU.mult, op1=ALU.add).then_inc(y_read, 1)
                dve.wait_ge(y_read, START + b + 1)
                layer_norm(pre2, steps, var2_ready, std2_ready, b, ln2_g_bc, ln2_b_bc, pre2).then_inc(out_ready, 1)
                assert steps.n == 4

            def experts_and_retrieval(b, t, r, b5=None):
                steps = Steps(dve, topk_step, r * TOPK_STEPS, consts)
                for g in range(TOPK // 2):
                    dots(b, t, g)
                    if g == 2:
                        wait_alone(dve, score_ready, START + r + 1, consts)
                        topk_half(steps, 0)
                    if g == 3:
                        topk_half(steps, 1)
                    if g == 4:
                        topk_pairs(steps, r)
                    if g == 5:
                        expert_index(steps, r)
                softmax(r)
                assert steps.n == TOPK_STEPS
                if b5 is not None:
                    x1_block(b5)

            dve.wait_ge(rows_in, 48)
            x1_block(0)
            dve.wait_ge(x1_ready, START + 1)
            steps = Steps(dve, topk_step)
            dve.wait_ge(score_ready, START + 1)
            topk_half(steps, 0)
            topk_half(steps, 1)
            topk_pairs(steps, 0)
            expert_index(steps, 0)
            assert steps.n == TOPK_STEPS, steps.n
            softmax(0)
            with dve.Fori(0, PH - 1) as h:
                experts_and_retrieval(0, h, h + 1, h + 1)
            dve.wait_ge(x1_ready, START + NB)
            experts_and_retrieval(0, PH - 1, PH)
            dve.wait_ge(rows2_in, 32)
            finish(0)
            with dve.Fori(1, NB - 1) as b:
                with dve.Fori(0, PH) as h:
                    experts_and_retrieval(b, b * PH + h, b * PH + h + 1)
                finish(b)
            with dve.Fori(0, PH - 1) as h:
                experts_and_retrieval(NB - 1, h + (NB - 1) * PH, h + ((NB - 1) * PH + 1))
            for g in range(TOPK // 2):
                dots(NB - 1, NB * PH - 1, g)
            finish(NB - 1)


def kernel(x, w_in, b_in, conv_w_dw, conv_b_dw, conv_ln_g, conv_ln_b, conv_w_pw2, conv_b_pw2, sb_w_o,
           w_out, b_out, ln1_g, ln1_b, peer_w_q, peer_keys_1, peer_keys_2, peer_u, peer_v, ln2_g, ln2_b):
    import numpy as np
    import concourse.bacc as bacc
    from concourse.bass_utils import run_bass_kernel_spmd

    def arr(a):
        return np.asarray(a)[0]

    x2, wi, bi = arr(x), arr(w_in), arr(b_in)
    col_q, col_k, col_v, col_g = 1024, 1536, 2048, 2560

    def ktile(w):
        return w.reshape(w.shape[0] // P, P, w.shape[1]).transpose(1, 0, 2)

    def slab(w, c):
        return ktile(w[:, c:c + P]).reshape(P, w.shape[0])

    def col(v):
        return v.reshape(-1, P).T

    order = []
    for c in range(CC):
        order += [c * P, CONV + c * P, col_q + c * P, col_k + c * P]
    taps = arr(conv_w_dw).T.reshape(CC, P, TAPS).transpose(1, 0, 2).reshape(P, CC * TAPS)
    data = {
        "xT": ktile(x2.T),
        "x": x2,
        "w_proj": np.stack([slab(wi, c) for c in order]),
        "w_v": ktile(wi[:, col_v:col_g]),
        "w_mix": np.stack([np.concatenate([slab(wi, col_g + m * P), slab(wi, col_g + D + m * P),
                                           slab(arr(conv_w_pw2), m * P), slab(arr(sb_w_o), m * P)], axis=1)
                           for m in range(KD)]),
        "w_out": ktile(arr(w_out)),
        "w_q": ktile(arr(peer_w_q)).reshape(P, KD, PH, 2 * P).transpose(0, 2, 1, 3),
        "keys": np.stack([arr(peer_keys_1), arr(peer_keys_2)], axis=1).transpose(3, 0, 1, 2).reshape(P, PH * 2 * NKEY),
        "uv": np.concatenate([arr(peer_u), arr(peer_v)], axis=1),
        "cols": np.concatenate([col(bi[0:col_v]), col(bi[col_g:]), col(arr(conv_b_pw2)), col(arr(conv_b_dw)),
                                col(arr(conv_ln_g)), col(arr(conv_ln_b)), taps], axis=1),
        "bv": bi[col_v:col_g].reshape(1, -1),
        "b_out": arr(b_out), "ln1_g": arr(ln1_g), "ln1_b": arr(ln1_b), "ln2_g": arr(ln2_g), "ln2_b": arr(ln2_b),
    }
    nc = bacc.Bacc("TRN2", target_bir_lowering=False, num_devices=1)
    arrays, aps = {}, []
    for name, a in data.items():
        a = np.ascontiguousarray(a)
        arrays[f"{name}_dram"] = a
        aps.append(nc.dram_tensor(f"{name}_dram", a.shape, mybir.dt.from_np(a.dtype), kind="ExternalInput").ap())
    out = nc.dram_tensor("out_dram", (S, D), F32, kind="ExternalOutput").ap()
    build(nc, *aps, out)
    r = run_bass_kernel_spmd(nc, [arrays], core_ids=[0])
    return r.results[0]["out_dram"].reshape(1, S, D)
```
